# Optimizing a Trainium2 kernel written in Bass

```python
import jax, jax.numpy as jnp
from jax import lax
import numpy as np

D_MODEL = 1024
BATCH = 1
SEQ = 512
DEPTH = 2

N_A_LAYERS = DEPTH // 2
N_B_LAYERS = DEPTH - N_A_LAYERS
D_FF = 2816
RMS_EPS = 1e-6

RWKV_HEAD_DIM = 64
RWKV_HEADS = D_MODEL // RWKV_HEAD_DIM
D_DECAY_LORA = 64
D_AAA_LORA = 64
D_MV_LORA = 32
D_GATE_LORA = 64
GN_EPS = 64e-5

DIL_GROUPS = ((128, 1), (512, 4), (2048, 16))
N_GROUPS = len(DIL_GROUPS)
ATTN_HEAD_DIM = 64
ATTN_HEADS = D_MODEL // ATTN_HEAD_DIM
Q_WIDTH = N_GROUPS * ATTN_HEADS * ATTN_HEAD_DIM
NEG_INF = -1e30

kernel_name = "rwkv7_yoco_dilated_macaron"

def rms_norm(x, g):
    xf = x.astype(jnp.float32)
    y = xf * lax.rsqrt(jnp.mean(xf * xf, axis=-1, keepdims=True) + RMS_EPS)
    return (y * g.astype(jnp.float32)).astype(x.dtype)

def swiglu(h, w_in, w_out):
    gate, up = jnp.split(h @ w_in, 2, axis=-1)
    return (jax.nn.silu(gate) * up) @ w_out

def token_shift(x):
    return jnp.pad(x, ((0, 0), (1, 0), (0, 0)))[:, :-1]

def rwkv7_recurrence(r, decay, k, v, a, b):
    Bsz, T, H, N = r.shape

    def step(S, inp):
        r_t, w_t, k_t, v_t, a_t, b_t = inp
        sa = jnp.einsum('bhij,bhj->bhi', S, a_t)
        S = S * w_t[:, :, None, :] + sa[..., None] * b_t[:, :, None, :] + v_t[..., None] * k_t[:, :, None, :]
        y = jnp.einsum('bhij,bhj->bhi', S, r_t)
        return S, y

    xs = tuple(jnp.moveaxis(t.astype(jnp.float32), 1, 0) for t in (r, decay, k, v, a, b))
    S0 = jnp.zeros((Bsz, H, N, N), jnp.float32)
    _, ys = lax.scan(step, S0, xs)
    return jnp.moveaxis(ys, 0, 1)

def rwkv7_time_mix(h, v_first, vres, mu, w_rkv, w0, w1, w2, a0, a1, a2, g1, g2,
                   k_k, k_a, r_k, ln_w, ln_b, w_o):
    Bsz, T, C = h.shape
    heads = lambda t: t.reshape(Bsz, T, RWKV_HEADS, RWKV_HEAD_DIM)
    xx = token_shift(h) - h
    xr, xw, xk, xv, xa, xg = [h + xx * mu[j] for j in range(6)]
    r = xr @ w_rkv[0]
    k = xk @ w_rkv[1]
    v = xv @ w_rkv[2]
    w = -jax.nn.softplus(-(w0 + jnp.tanh(xw @ w1) @ w2)) - 0.5
    decay = jnp.exp(-jnp.exp(w.astype(jnp.float32)))
    if vres is None:
        v_first = v
    else:
        v0, v1, v2 = vres
        v = v + (v_first - v) * jax.nn.sigmoid(v0 + (xv @ v1) @ v2)
    a = jax.nn.sigmoid(a0 + (xa @ a1) @ a2)
    g = jax.nn.sigmoid(xg @ g1) @ g2
    kk = heads(k * k_k).astype(jnp.float32)
    kk = kk / jnp.maximum(jnp.linalg.norm(kk, axis=-1, keepdims=True), 1e-12)
    k = k * (1.0 + (a - 1.0) * k_a)
    rh, kh, vh = heads(r), heads(k), heads(v)
    y = rwkv7_recurrence(rh, heads(decay), kh, vh, -kk, kk * heads(a))
    mean = jnp.mean(y, axis=-1, keepdims=True)
    var = jnp.mean(jnp.square(y - mean), axis=-1, keepdims=True)
    y = ((y - mean) * lax.rsqrt(var + GN_EPS)).reshape(Bsz, T, C) * ln_w + ln_b
    bonus = jnp.sum(rh * kh * r_k, axis=-1, keepdims=True) * vh
    y = y.astype(h.dtype) + bonus.reshape(Bsz, T, C)
    return (y * g) @ w_o, v_first

def dilated_group_attention(q, k, v, window, dilation):
    Bsz, T, H, Dh = q.shape
    blk = window // dilation
    Tp = -(-T // window) * window
    M = Tp // dilation
    NB = M // blk

    def to_blocks(t):
        t = jnp.pad(t, ((0, 0), (0, Tp - T), (0, 0), (0, 0)))
        t = t.reshape(Bsz, M, dilation, H, Dh).transpose(0, 2, 1, 3, 4)
        return t.reshape(Bsz, dilation, NB, blk, H, Dh)

    def with_prev(t):
        prev = jnp.pad(t, ((0, 0), (0, 0), (1, 0), (0, 0), (0, 0), (0, 0)))[:, :, :-1]
        return jnp.concatenate([prev, t], axis=3)

    def from_blocks(t):
        t = t.reshape((Bsz, dilation, M) + t.shape[4:])
        t = jnp.swapaxes(t, 1, 2).reshape((Bsz, Tp) + t.shape[3:])
        return t[:, :T]

    qb, kb, vb = to_blocks(q), to_blocks(k), to_blocks(v)
    ks, vs = with_prev(kb), with_prev(vb)
    s = jnp.einsum('brnqhd,brnkhd->brnhqk', qb, ks).astype(jnp.float32)
    qi = jnp.arange(blk)[:, None]
    kj = jnp.arange(2 * blk)[None, :]
    band = (kj >= qi) & (kj <= qi + blk)
    mask = band[None] & ((jnp.arange(NB)[:, None, None] > 0) | (kj >= blk)[None])
    s = jnp.where(mask[None, None, :, None], s, NEG_INF)
    m = jnp.max(s, axis=-1, keepdims=True)
    p = jnp.exp(s - m)
    l = jnp.sum(p, axis=-1, keepdims=True)
    o = jnp.einsum('brnhqk,brnkhd->brnqhd', p / l, vs.astype(jnp.float32))
    lse = jnp.swapaxes((m + jnp.log(l))[..., 0], -1, -2)
    return from_blocks(o), from_blocks(lse)

def shared_kv(x, kv_norm, w_kv, k_gain):
    Bsz, T, _ = x.shape
    kv = (rms_norm(x, kv_norm) @ w_kv).reshape(Bsz, T, 2, N_GROUPS, ATTN_HEADS, ATTN_HEAD_DIM)
    k = rms_norm(kv[:, :, 0], k_gain[:, None, :])
    return k, kv[:, :, 1]

def dilated_attention_mixer(h, k_sh, v_sh, w_q, q_gain, w_o):
    Bsz, T, _ = h.shape
    q = (h @ w_q).reshape(Bsz, T, N_GROUPS, ATTN_HEADS, ATTN_HEAD_DIM)
    q = rms_norm(q, q_gain[:, None, :]) * ATTN_HEAD_DIM ** -0.5
    outs, lses = [], []
    for g, (win, dil) in enumerate(DIL_GROUPS):
        o, lse = dilated_group_attention(q[:, :, g], k_sh[:, :, g], v_sh[:, :, g], win, dil)
        outs.append(o)
        lses.append(lse)
    alpha = jax.nn.softmax(jnp.stack(lses, axis=0), axis=0)
    o = jnp.sum(alpha[..., None] * jnp.stack(outs, axis=0), axis=0)
    return o.reshape(Bsz, T, ATTN_HEADS * ATTN_HEAD_DIM).astype(h.dtype) @ w_o

def setup_inputs(seed: int = 0) -> dict:
    key = jax.random.key(seed)
    ks = iter(jax.random.split(key, 40))
    f32 = jnp.float32
    D, F, NA, NB = D_MODEL, D_FF, N_A_LAYERS, N_B_LAYERS
    H, N = RWKV_HEADS, RWKV_HEAD_DIM

    def nrm(shape, scale):
        return jax.random.normal(next(ks), shape, f32) * scale

    def gain(shape):
        return 1.0 + nrm(shape, 0.02)

    def unif(shape, lo, hi):
        return jax.random.uniform(next(ks), shape, f32, lo, hi)

    return {
        "x": nrm((BATCH, SEQ, D), 1.0),
        "ffn_norm": gain((DEPTH, 2, D)),
        "ffn_w_in": nrm((DEPTH, 2, D, 2 * F), D ** -0.5),
        "ffn_w_out": nrm((DEPTH, 2, F, D), F ** -0.5),
        "mix_norm": gain((DEPTH, D)),
        "rwkv_mu": unif((NA, 6, D), 0.0, 1.0),
        "rwkv_w_rkv": nrm((NA, 3, D, D), D ** -0.5),
        "rwkv_w0": unif((NA, D), -5.0, -1.0),
        "rwkv_w1": nrm((NA, D, D_DECAY_LORA), D ** -0.5),
        "rwkv_w2": nrm((NA, D_DECAY_LORA, D), 0.1 * D_DECAY_LORA ** -0.5),
        "rwkv_a0": nrm((NA, D), 0.1),
        "rwkv_a1": nrm((NA, D, D_AAA_LORA), D ** -0.5),
        "rwkv_a2": nrm((NA, D_AAA_LORA, D), 0.5 * D_AAA_LORA ** -0.5),
        "rwkv_v0": 1.0 + nrm((NA - 1, D), 0.1),
        "rwkv_v1": nrm((NA - 1, D, D_MV_LORA), D ** -0.5),
        "rwkv_v2": nrm((NA - 1, D_MV_LORA, D), 0.5 * D_MV_LORA ** -0.5),
        "rwkv_g1": nrm((NA, D, D_GATE_LORA), D ** -0.5),
        "rwkv_g2": nrm((NA, D_GATE_LORA, D), D_GATE_LORA ** -0.5),
        "rwkv_k_k": 0.85 + nrm((NA, D), 0.05),
        "rwkv_k_a": 1.0 + nrm((NA, D), 0.05),
        "rwkv_r_k": nrm((NA, H, N), 0.1),
        "rwkv_ln_w": gain((NA, D)),
        "rwkv_ln_b": nrm((NA, D), 0.02),
        "rwkv_w_o": nrm((NA, D, D), D ** -0.5),
        "kv_norm": gain((D,)),
        "w_kv": nrm((D, 2 * Q_WIDTH), D ** -0.5),
        "k_norm": gain((N_GROUPS, ATTN_HEAD_DIM)),
        "attn_w_q": nrm((NB, D, Q_WIDTH), D ** -0.5),
        "q_norm": gain((NB, N_GROUPS, ATTN_HEAD_DIM)),
        "attn_w_o": nrm((NB, ATTN_HEADS * ATTN_HEAD_DIM, D), (ATTN_HEADS * ATTN_HEAD_DIM) ** -0.5),
    }

def reference(x, ffn_norm, ffn_w_in, ffn_w_out, mix_norm, rwkv_mu, rwkv_w_rkv, rwkv_w0,
              rwkv_w1, rwkv_w2, rwkv_a0, rwkv_a1, rwkv_a2, rwkv_v0, rwkv_v1, rwkv_v2,
              rwkv_g1, rwkv_g2, rwkv_k_k, rwkv_k_a, rwkv_r_k, rwkv_ln_w, rwkv_ln_b, rwkv_w_o,
              kv_norm, w_kv, k_norm, attn_w_q, q_norm, attn_w_o):
    v_first = None
    k_sh = None
    v_sh = None
    for l in range(DEPTH):
        x = x + 0.5 * swiglu(rms_norm(x, ffn_norm[l, 0]), ffn_w_in[l, 0], ffn_w_out[l, 0])
        h = rms_norm(x, mix_norm[l])
        if l < N_A_LAYERS:
            vres = None if l == 0 else (rwkv_v0[l - 1], rwkv_v1[l - 1], rwkv_v2[l - 1])
            y, v_first = rwkv7_time_mix(h, v_first, vres, rwkv_mu[l], rwkv_w_rkv[l], rwkv_w0[l],
                                        rwkv_w1[l], rwkv_w2[l], rwkv_a0[l], rwkv_a1[l], rwkv_a2[l],
                                        rwkv_g1[l], rwkv_g2[l], rwkv_k_k[l], rwkv_k_a[l], rwkv_r_k[l],
                                        rwkv_ln_w[l], rwkv_ln_b[l], rwkv_w_o[l])
        else:
            i = l - N_A_LAYERS
            y = dilated_attention_mixer(h, k_sh, v_sh, attn_w_q[i], q_norm[i], attn_w_o[i])
        x = x + y
        x = x + 0.5 * swiglu(rms_norm(x, ffn_norm[l, 1]), ffn_w_in[l, 1], ffn_w_out[l, 1])
        if l == N_A_LAYERS - 1:
            k_sh, v_sh = shared_kv(x, kv_norm, w_kv, k_norm)
    return x


_drawn_inputs = setup_inputs


def setup_inputs(seed=0):
    import zlib

    import numpy as np

    out = dict(_drawn_inputs(seed))
    spreads = {}
    factors = {'ffn_norm': 3.323,
     'mix_norm': 2.884,
     'rwkv_w1': 8.0,
     'rwkv_w2': 8.0,
     'rwkv_k_k': 3.06,
     'rwkv_ln_w': 5.329,
     'rwkv_ln_b': 5.223,
     'kv_norm': 8.0,
     'k_norm': 8.0,
     'q_norm': 8.0}
    for name, (base, spread) in spreads.items():
        noise = np.random.default_rng([zlib.crc32(name.encode()), seed]).standard_normal(out[name].shape)
        drawn = base * np.exp(spread * noise) if base else spread * noise
        out[name] = __import__('jax').numpy.asarray(drawn.astype(out[name].dtype))
    for name, factor in factors.items():
        out[name] = (out[name] * factor).astype(out[name].dtype)
    return out
```

```python
from contextlib import ExitStack

import numpy as np

import concourse.bass as bass
from concourse import mybir

F32 = mybir.dt.float32
F32R = mybir.dt.float32r
ALU = mybir.AluOpType
ACT = mybir.ActivationFunctionType
AX = mybir.AxisListType
BF16 = mybir.dt.bfloat16
NEG = -1e30

P = 128
SLOTS = 4
LEAD = SLOTS - 1
CHUNK = 1024


KV_PHASE = 3
MIXER_SMALL = 16960


def rwkv_steps(pairs, levels, chunks):
    steps = []
    for q in range(pairs):
        steps += [("pre", q, 0), ("units", q, 0)] + [("level", q, l) for l in range(1, levels)]
        steps += [("scan", q, c) for c in range(chunks)] + [("post", q, 0)]
    return steps


def build(nc, a, out, lo=0, upto=99):
    x_in = a["x"]
    _, T, D = x_in.shape
    KT = D // P
    FF = a["ffn_w_out"].shape[2]
    FT = FF // P
    TB = T // P
    EPS = 1e-6
    GROUPS = FT // 2
    G_CHUNKS = KT // 2
    FFN_CHUNKS = GROUPS * G_CHUNKS + FT
    assert T == 512 and D == 1024 and FT % 2 == 0 and GROUPS % 2 == 1 and (FT - 2) % SLOTS == 0

    ctx = ExitStack()
    with ctx:
        def sb(name, shape, dt=F32):
            return ctx.enter_context(nc.sbuf_tensor(name, shape, dt))

        def sem(name):
            return ctx.enter_context(nc.semaphore(name))

        GN_EPS = 64e-5
        bank = [ctx.enter_context(nc.psum_tensor(f"bank{i}", [P, 512], F32)) for i in range(8)]

        def tensors(stack, **shapes):
            return [stack.enter_context(nc.sbuf_tensor(n, [P, *sh], dt)) for n, (sh, dt) in shapes.items()]

        CH, HD = 64, 64
        NC, UNITS = T // CH, 2 * TB
        x, w_hi, ident, ones, par, stat = tensors(
            ctx, x=((KT, T), F32), w_hi=((SLOTS, CHUNK), F32R), ident=((P,), F32), ones=((P,), F32),
            par=((232,), F32), stat=((4, 16), F32))
        with ExitStack() as c:
            am, inv_x, inv_g = tensors(c, am=((2, UNITS, 4 * P), F32), inv_x=((2, 4, P), F32), inv_g=((2, 4, P), F32))
        w_raw, w_lo, square, ssq, rstd, diag = tensors(
            ctx, w_raw=((SLOTS, CHUNK), F32), w_lo=((SLOTS, CHUNK), F32R), square=((2, T), F32), ssq=((T,), F32),
            rstd=((T,), F32), diag=((TB, P), F32))
        with ExitStack() as c:
            xg_hi, xg_lo, hid_hi, hid_lo, gate, up = tensors(
                c, xg_hi=((KT, T), F32R), xg_lo=((KT, T), F32R), hid_hi=((FT, T), F32R), hid_lo=((FT, T), F32R),
                gate=((2, T), F32), up=((2, T), F32))
        with ExitStack() as c:
            x_rows, par_rows = tensors(c, x_rows=((TB, D), F32), par_rows=((2, P), F32))
        with ExitStack() as c:
            with ExitStack() as c1:
                h, mixed, mix_hi, mix_lo, lora1 = tensors(
                    c1, h=((KT, T + 1), F32), mixed=((4, T), F32), mix_hi=((4, T), F32R), mix_lo=((4, T), F32R),
                    lora1=((3, KT, HD), F32))
            with ExitStack() as c2:
                (inv_u, ar, btok, ktok, pcum, dec, bt, kt, kkr, sqt, rk, vt, bonus_v, ys, spread_t, unit_mask, level_mask,
                 head_ones, head_mean, head_mask, cst, pend, state, decayed, zs, sas) = tensors(
                    c2, inv_u=((2, UNITS, P), F32), ar=((2, 2, 2, T), F32), btok=((2, T), F32), ktok=((2, T), F32),
                    pcum=((NC, CH + 1), F32), dec=((T,), F32), bt=((T,), F32), kt=((T,), F32), kkr=((T,), F32),
                    sqt=((T,), F32), rk=((T,), F32), vt=((T,), F32), bonus_v=((2, T), F32), ys=((T,), F32),
                    spread_t=((8, HD), F32), unit_mask=((4 * P,), F32), level_mask=((6, P), F32), head_ones=((P,), F32),
                    head_mean=((P,), F32), head_mask=((4,), F32), cst=((6, 8), F32), pend=((2, NC), F32),
                    state=((2, HD), F32), decayed=((HD,), F32), zs=((2 * HD,), F32), sas=((2 * HD,), F32))
            tensors(c, both=((MIXER_SMALL,), F32))
            with ExitStack() as c3:
                y_hi, y_lo = tensors(c3, y_hi=((KT, T), F32R), y_lo=((KT, T), F32R))
            k_all, r_all, v_all, lora_u, lora2 = tensors(
                c, k_all=((KT, T), F32), r_all=((KT, T), F32), v_all=((TB, D), F32), lora_u=((3, T), F32),
                lora2=((2, D), F32))

        NG = a["k_norm"].shape[0]
        HEADS = D // HD
        with ExitStack() as c:
            with ExitStack() as c1:
                tensors(c1, xg_place=((2 * KT, T), F32))
            with ExitStack() as c2:
                keys, values, probs = tensors(
                    c2, keys=((2, NG, T), F32), values=((2, NG, TB, P), F32), probs=((2, TB, 2 * P), F32))
            with ExitStack() as c3:
                (spread_w,) = tensors(c3, spread_w=((2, 2, TB, 2, HD), F32))
            _, q_all = tensors(c, xg_again=((2 * KT, T), F32), q_all=((KT, NG, T), F32))
            with ExitStack() as c4:
                stage, raw, raw_sq, group_stat = tensors(
                    c4, stage=((2, 4, T), F32), raw=((TB, T), F32), raw_sq=((2, T), F32), group_stat=((4, 8 * TB), F32))
            with ExitStack() as c5:
                q_pad, probs_t = tensors(c5, q_pad=((2, NG, 2, T), F32), probs_t=((2, 2 * TB, P), F32))
            with ExitStack() as c6:
                (o_hl,) = tensors(c6, o_hl=((KT, 2, T), F32R))
            (_, masks_f, masks_bf, ident_bf, select, onehot, penalty, head_half, sums, picked, turned, joint) = tensors(
                c, o_again=((KT, 2, T), F32), masks_f=((3, P), F32), masks_bf=((4, T), BF16), ident_bf=((P,), BF16),
                select=((TB, P), F32), onehot=((TB,), F32), penalty=((TB,), F32), head_half=((2,), F32),
                sums=((2, TB, 2, HEADS), F32), picked=((TB, 2 * HEADS, TB), F32), turned=((TB, 2 * HEADS), F32),
                joint=((8, TB, HEADS), F32))
        k_dram = nc.dram_tensor("k_dram", (NG, KT, P, T), F32, kind="Internal").ap()
        v_dram = nc.dram_tensor("v_dram", (NG, TB, P, D), F32, kind="Internal").ap()

        PAR = {}
        vectors = []
        for l in range(2):
            for s in range(2):
                vectors.append((f"ffn{l}{s}", a["ffn_norm"][l, s]))
        for l in range(2):
            vectors.append((f"mix{l}", a["mix_norm"][l]))
        for j in range(6):
            vectors.append((f"mu{j}", a["rwkv_mu"][0, j]))
        for name in ("kv_norm", "rwkv_w0", "rwkv_a0", "rwkv_k_k", "rwkv_k_a", "rwkv_r_k", "rwkv_ln_w", "rwkv_ln_b"):
            v = a[name]
            if name == "rwkv_r_k":
                v = v[0].rearrange("h n -> (h n)")
            elif name != "kv_norm":
                v = v[0]
            vectors.append((name, v))
        for i, (name, _) in enumerate(vectors):
            PAR[name] = i * KT
        ROWS_A = P // KT

        def col(name, k):
            return par[:, PAR[name] + k:PAR[name] + k + 1]

        PAR_QK = len(vectors) * KT
        PAR_EXT = PAR_QK + 2 * NG

        h_pad = sem("h_pad")
        h_ready = sem("h_ready")
        ext_ready = sem("ext_ready")
        lora_zero = sem("lora_zero")
        lora_landed = sem("lora_landed")
        lora_ready = sem("lora_ready")
        shift_scaled = sem("shift_scaled")
        mix_ready = sem("mix_ready")
        mix_used = sem("mix_used")
        mix_hi_ready = sem("mix_hi_ready")
        mix_lo_ready = sem("mix_lo_ready")
        projected = sem("projected")
        projection_copied = sem("projection_copied")
        mask_step = sem("mask_step")
        masks_ready = sem("masks_ready")
        work_done = sem("work_done")
        work_read = [sem(f"work_read{i}") for i in range(2)]
        EVENTS = dict(
            undecay=1, decay=1, kkr=1, sq=1, scan_p=NC, scan_r=NC, floor=1, inv=1, spread_pre=1, tk=1, kp=1, kka=1, bt=1,
            kt=1, ar=4, pend=1, rk=1, firstm=2, first=2, t=10, x=10, g=10, gs=10, u=10, us=10, z=NC, zs=NC, sa=NC, sas=NC,
            st=NC - 1, decayed=NC - 2, state=NC - 1, y=NC, ys=1, ysq=1, ginv=1, groot=1, spread_post=1, yl=1, biased=1,
            y_hi=1, y_lo=1)
        S = {name: sem(f"rwkv_{name}") for name in EVENTS}
        par_landed = sem("par_landed")
        x_landed = [sem(f"x_landed{b}") for b in range(TB)]
        par_turned = sem("par_turned")
        par_ready = sem("par_ready")
        x_turned = sem("x_turned")
        id_zero = sem("id_zero")
        const_ready = sem("const_ready")
        w_landed = [[sem(f"w_landed{i}_{h}") for h in range(2)] for i in range(SLOTS)]
        w_hi_ready = sem("w_hi_ready")
        w_lo_ready = sem("w_lo_ready")
        w_used = sem("w_used")
        x_new = sem("x_new")
        sq_ready = sem("sq_ready")
        ssq_ready = sem("ssq_ready")
        xg_hi_ready = sem("xg_hi_ready")
        xg_lo_ready = sem("xg_lo_ready")
        ms_ready = sem("ms_ready")
        var_ready = sem("var_ready")
        inv_ready = sem("inv_ready")
        root_ready = sem("root_ready")
        diag_ready = sem("diag_ready")
        spread_done = sem("spread_done")
        rstd_ready = sem("rstd_ready")
        gate_scaled = sem("gate_scaled")
        up_scaled = sem("up_scaled")
        silu_done = sem("silu_done")
        hid_done = sem("hid_done")
        hid_hi_ready = sem("hid_hi_ready")
        hid_lo_ready = sem("hid_lo_ready")
        out_done = sem("out_done")
        y_turned = sem("y_turned")
        y_ready = sem("y_ready")
        y_right_ready = sem("y_right_ready")
        y_stored = sem("y_stored")
        stored = [sem(f"stored{i}") for i in range(2)]
        keys_landed = [[sem(f"keys_landed{i}_{g}") for g in range(3)] for i in range(2)]
        values_landed = [[sem(f"values_landed{i}_{g}") for g in range(3)] for i in range(2)]
        (staged_even, staged_odd, v_even, v_odd, group_normed, group_turned, group_raw, group_squared, group_summed,
         group_inv, group_var, group_root, gains_ready, attn_mask_step, attn_const, negmax_ready, q_padded,
         scores_done, p_ready, pv_done, converted, merged, exps_ready, weights_ready,
         w_spread, weighted, o_hi_ready, o_lo_ready, spread_source, picked_done) = [sem(n) for n in (
             "staged_even", "staged_odd", "v_even", "v_odd", "group_normed", "group_turned", "group_raw",
             "group_squared", "group_summed", "group_inv", "group_var", "group_root", "gains_ready", "attn_mask_step",
             "attn_const", "negmax_ready", "q_padded", "scores_done", "p_ready", "pv_done", "converted", "merged",
             "exps_ready", "weights_ready", "w_spread", "weighted", "o_hi_ready", "o_lo_ready", "spread_source", "picked_done")]
        u_copied = [sem(f"u_copied{f}") for f in range(2)]
        turn_done = [sem(f"turn_done{i}") for i in range(2)]
        turn_read = [sem(f"turn_read{i}") for i in range(2)]

        def plus(const, i, step):
            return const if i is None else i * step + const

        def load_chunk(sp, c, halves, i=None, step=0):
            s = c % SLOTS
            if i is not None or c >= SLOTS:
                sp.wait_ge(w_lo_ready, plus(c - SLOTS + 1, i, step))
            for h, (src, place) in enumerate(halves):
                sp.dma_start(place(w_raw[:, s, :]), src).then_inc(w_landed[s][h], 16)

        def row_halves(src):
            return [(src[:, h * 512:(h + 1) * 512], lambda slot, h=h: slot[:, h * 512:(h + 1) * 512])
                    for h in range(2)]

        def column_halves(srcs):
            return [(src, lambda slot, h=h: slot.rearrange("p (kt n) -> p kt n", kt=2)[:, :, h * 256:(h + 1) * 256])
                    for h, src in enumerate(srcs)]

        def split_hi(act, c, i=None, step=0):
            s = c % SLOTS
            for h in range(2):
                act.wait_ge(w_landed[s][h], plus((c // SLOTS + 1) * 16, i, step * 16 // SLOTS))
            if i is not None or c >= SLOTS:
                act.wait_ge(w_used, plus(c - SLOTS + 1, i, step))
            act.activation(w_hi[:, s, :], w_raw[:, s, :], ACT.Copy).then_inc(w_hi_ready, 1)

        def split_lo(pool, c, i=None, step=0):
            s = c % SLOTS
            pool.wait_ge(w_hi_ready, plus(c + 1, i, step))
            pool.tensor_tensor(w_lo[:, s, :], w_raw[:, s, :], w_hi[:, s, :].bitcast(F32),
                               ALU.subtract).then_inc(w_lo_ready, 1)

        def split_hi_run(act, c, n):
            if n >= 2 * SLOTS:
                with act.Fori(0, n // SLOTS) as i:
                    for u in range(SLOTS):
                        split_hi(act, c + u, i, SLOTS)
                c, n = c + n // SLOTS * SLOTS, n % SLOTS
            for u in range(n):
                split_hi(act, c + u)

        def split_lo_run(pool, c, n):
            if n >= 2 * SLOTS:
                with pool.Fori(0, n // SLOTS) as i:
                    for u in range(SLOTS):
                        split_lo(pool, c + u, i, SLOTS)
                c, n = c + n // SLOTS * SLOTS, n % SLOTS
            for u in range(n):
                split_lo(pool, c + u)

        def products(pe, o, s, w0, x_hi, x_lo, start, stop):
            hi, lo = w_hi[:, s, w0:w0 + P], w_lo[:, s, w0:w0 + P]
            pe.matmul(o, hi, x_hi, start=start, stop=False)
            pe.matmul(o, hi, x_lo, start=False, stop=False)
            return pe.matmul(o, lo, x_hi, start=False, stop=stop)

        def products_turned(pe, o, s, w0, x_hi, x_lo, start, stop):
            hi, lo = w_hi[:, s, w0:w0 + 512], w_lo[:, s, w0:w0 + 512]
            pe.matmul(o, x_hi, hi, start=start, stop=False)
            pe.matmul(o, x_lo, hi, start=False, stop=False)
            return pe.matmul(o, x_hi, lo, start=False, stop=stop)

        def update_dve(dve, ph):
            u, p, st = ph["update"], ph["prep"], ph["stat"]

            def new_x(m):
                if u == 0:
                    dve.wait_ge(x_turned, m + 1)
                    dve.tensor_copy(x[:, m], bank[m][:, :]).then_inc(x_new, 1)
                    return
                if m < KT - 1:
                    dve.wait_ge(out_done, (KT - 1) * (u - 1) + m + 1)
                else:
                    dve.wait_ge(w_used, ph["c0"])
                dve.scalar_tensor_tensor(x[:, m], bank[m][:, :], ph["scale"], x[:, m],
                                         ALU.mult, ALU.add).then_inc(x_new, 1)

            def low(m):
                dve.wait_ge(xg_hi_ready, KT * p + m + 1)
                dve.scalar_tensor_tensor(xg_lo[:, m], x[:, m], col(ph["gain"], m), xg_hi[:, m].bitcast(F32),
                                         ALU.mult, ALU.subtract).then_inc(xg_lo_ready, 1)

            def add_squares(m):
                dve.wait_ge(sq_ready, KT * st + m + 1)
                if m == 0:
                    dve.tensor_copy(ssq[:, :], square[:, 0]).then_inc(ssq_ready, 1)
                    return
                dve.wait_ge(ssq_ready, KT * st + m)
                dve.tensor_tensor(ssq[:, :], ssq[:, :], square[:, m % 2], ALU.add).then_inc(ssq_ready, 1)

            if u is not None:
                for m in range(4):
                    new_x(m)
                if u == 0:
                    dve.wait_ge(par_ready, 2)
            for m in range(KT):
                if p is not None:
                    low(m)
                if u is not None and m + 4 < KT:
                    new_x(m + 4)
                if st is not None:
                    add_squares(m)

        def update_act(act, ph):
            u, p, st = ph["x"], ph["prep"], ph["stat"]
            if ph["update"] is None:
                act.wait_ge(w_used, ph["c0"])
            for m in range(KT):
                act.wait_ge(x_new, KT * u + m + 1)
                if p is not None:
                    act.activation(xg_hi[:, m], x[:, m], ACT.Copy, scale=col(ph["gain"], m)).then_inc(xg_hi_ready, 1)
                if st is not None:
                    if KT * st + m >= 2:
                        act.wait_ge(ssq_ready, KT * st + m - 1)
                    act.activation(square[:, m % 2], x[:, m], ACT.Square).then_inc(sq_ready, 1)

        def mean_square_pe(pe, ph):
            pe.wait_ge(ssq_ready, KT * (ph["stat"] + 1))
            pe.wait_ge(x_new, KT * (ph["x"] + 1))
            for b in range(2 * TB):
                ts = slice(b * P, (b + 1) * P) if b < TB else slice(b - TB, T, TB)
                last = pe.matmul(bank[4][:, b:b + 1], ssq[:, ts], ones[:, 0:1], start=True, stop=True)
            last.then_inc(ms_ready, 1)

        def spread_pe(pe, ph):
            pe.wait_ge(diag_ready, TB * (ph["stat"] + 1))
            for b in range(TB):
                last = pe.matmul(bank[5][:, b * P:(b + 1) * P], ones[:, :], diag[:, b], start=True, stop=True)
            last.then_inc(spread_done, 1)

        def rstd_dve(dve, ph):
            st = ph["stat"]
            dve.wait_ge(ms_ready, st + 1)
            dve.tensor_scalar(stat[:, 0, 0:2 * TB], bank[4][:, 0:2 * TB], 1.0 / D, EPS,
                              ALU.mult, ALU.add).then_inc(var_ready, 1)
            dve.wait_ge(var_ready, st + 1)
            dve.reciprocal(stat[:, 1, 0:2 * TB], stat[:, 0, 0:2 * TB]).then_inc(inv_ready, 1)
            dve.wait_ge(root_ready, st + 1)
            for b in range(TB):
                dve.tensor_scalar(diag[:, b], ident[:, :], stat[:, 2, b:b + 1], None,
                                  ALU.mult).then_inc(diag_ready, 1)
            dve.wait_ge(spread_done, st + 1)
            dve.tensor_copy(rstd[:, :], bank[5][:, :]).then_inc(rstd_ready, 1)

        def rstd_act(act, ph):
            act.wait_ge(inv_ready, ph["stat"] + 1)
            act.activation(stat[:, 2, 0:2 * TB], stat[:, 1, 0:2 * TB], ACT.Sqrt).then_inc(root_ready, 1)

        PAIRS = GROUPS // 2
        STEP = 2 * G_CHUNKS

        def peeled(ph):
            return int(ph["nth"] == 0)

        def ffn_load(sp, ph):
            n, c0 = ph["n"], ph["c0"]
            w_in = a["ffn_w_in"][n // 2, n % 2].rearrange("(kt p) (h n) -> p kt h n", p=P, h=2)
            w_out = a["ffn_w_out"][n // 2, n % 2]

            def group(c, g, i=None):
                for j in range(G_CHUNKS):
                    load_chunk(sp, c + j, column_halves([
                        w_in[:, 2 * j:2 * j + 2, h, bass.ds(g * 256, 256)] for h in range(2)]), i, STEP)

            group(c0, 0)
            if ph["update"] is None:
                for gi in range(len(KV_GROUPS) - 2, len(KV_GROUPS)):
                    store_group(sp, plan[KV_PHASE - lo], gi)
            with sp.Fori(0, PAIRS) as i:
                for u in range(2):
                    group(c0 + G_CHUNKS * (u + 1), i * 2 + (u + 1), i)
            c1 = c0 + GROUPS * G_CHUNKS
            load_chunk(sp, c1, row_halves(w_out[0:P, :]))
            with sp.Fori(0, (FT - 2) // SLOTS) as i:
                for u in range(SLOTS):
                    load_chunk(sp, c1 + 1 + u, row_halves(w_out[bass.ds(i * (SLOTS * P) + (1 + u) * P, P), :]), i, SLOTS)
            load_chunk(sp, c1 + FT - 1, row_halves(w_out[(FT - 1) * P:FT * P, :]))

        def ffn_act(act, ph):
            n, c0 = ph["n"], ph["c0"]
            base = ph["nth"] * FT

            def silus(t, i=None):
                for f in range(2):
                    act.wait_ge(gate_scaled, plus(base + t + f + 1, i, 4))
                    act.activation(gate[:, f], gate[:, f], ACT.Silu).then_inc(silu_done, 1)
                for f in range(2):
                    act.wait_ge(hid_done, plus(base + t + f + 1, i, 4))
                    act.activation(hid_hi[:, bass.ds(plus(t + f, i, 4), 1), :], up[:, f:f + 1, :],
                                   ACT.Copy).then_inc(hid_hi_ready, 1)

            if ph["update"] is None:
                for i in range(2):
                    act.wait_ge(stored[i], 16 * (len(KV_GROUPS) // 2))
            def two_groups(i=None):
                for u in range(2):
                    for j in range(G_CHUNKS):
                        split_hi(act, c0 + LEAD + G_CHUNKS * u + j, i, STEP)
                    silus(2 * u, i)

            if peeled(ph):
                two_groups()
            with act.Fori(peeled(ph), PAIRS) as i:
                two_groups(i)
            for j in range(G_CHUNKS):
                split_hi(act, c0 + LEAD + STEP * PAIRS + j)
            silus(FT - 2)
            c1 = c0 + LEAD + GROUPS * G_CHUNKS
            split_hi_run(act, c1, min(FT, CHUNKS - c1))

        def ffn_dve(dve, ph):
            n, c0 = ph["n"], ph["c0"]
            base = ph["nth"] * FT

            def evacuate(t, half, i=None):
                dve.wait_ge(w_used, plus(c0 + G_CHUNKS * (t // 2 + 1), i, STEP))
                for f in range(2):
                    dve.tensor_tensor(gate[:, f], bank[4 * half + f][:, :], rstd[:, :],
                                      ALU.mult).then_inc(gate_scaled, 1)
                for f in range(2):
                    if i is not None or base + t > 0:
                        dve.wait_ge(hid_lo_ready, plus(base + t, i, 4))
                    dve.tensor_tensor(up[:, f], bank[4 * half + 2 + f][:, :], rstd[:, :],
                                      ALU.mult).then_inc(up_scaled, 1)
                for f in range(2):
                    dve.wait_ge(silu_done, plus(base + t + f + 1, i, 4))
                    dve.wait_ge(up_scaled, plus(base + t + f + 1, i, 4))
                    dve.tensor_tensor(up[:, f], gate[:, f], up[:, f], ALU.mult).then_inc(hid_done, 1)
                for f in range(2):
                    dve.wait_ge(hid_hi_ready, plus(base + t + f + 1, i, 4))
                    tile = bass.ds(plus(t + f, i, 4), 1)
                    dve.tensor_tensor(hid_lo[:, tile, :], up[:, f:f + 1, :], hid_hi[:, tile, :].bitcast(F32),
                                      ALU.subtract).then_inc(hid_lo_ready, 1)

            dve.wait_ge(rstd_ready, ph["rstd"] + 1)
            if peeled(ph):
                for u in range(2):
                    evacuate(2 * u, u)
            with dve.Fori(peeled(ph), PAIRS) as i:
                for u in range(2):
                    evacuate(2 * u, u, i)
            evacuate(FT - 2, 0)

        def ffn_pool(pool, ph):
            c = ph["c0"] + LEAD
            split_lo_run(pool, c, min(FFN_CHUNKS, CHUNKS - c))

        def ffn_pe(pe, ph):
            n, c0 = ph["n"], ph["c0"]
            base = ph["nth"] * FT

            if ph["update"] is None:
                pe.wait_ge(v_even, 2 * KEYS_GROUPS)
                pe.wait_ge(v_odd, 2 * KEYS_GROUPS)

            def group(c, g, half, i=None, first=False):
                for j in range(G_CHUNKS):
                    s = (c + j) % SLOTS
                    pe.wait_ge(w_lo_ready, plus(c + j + 1, i, STEP))
                    if j == 0 and g > 0 and (i is not None or base + g > 1):
                        pe.wait_ge(up_scaled, plus(base + 2 * (g - 1), i, 4))
                    for kk in range(2):
                        k = 2 * j + kk
                        if first:
                            pe.wait_ge(xg_lo_ready, KT * ph["prep"] + k + 1)
                        for m in range(4):
                            if first and k == 0:
                                pe.wait_ge(x_new, KT * ph["x"] + m + 1)
                            last = products(pe, bank[4 * half + m][:, :], s, kk * 512 + m * P,
                                            xg_hi[:, k], xg_lo[:, k], k == 0, k == KT - 1)
                    last.then_inc(w_used, 1)
                    if first and ph["stat"] is not None:
                        if j == 2:
                            mean_square_pe(pe, ph)
                        if j == 3:
                            spread_pe(pe, ph)

            group(c0, 0, 0, first=True)
            pe.wait_ge(rstd_ready, ph["rstd"] + 1)
            if peeled(ph):
                for u in range(2):
                    group(c0 + G_CHUNKS * (u + 1), u + 1, 1 - u)
            with pe.Fori(peeled(ph), PAIRS) as i:
                for u in range(2):
                    group(c0 + G_CHUNKS * (u + 1), u + 1, 1 - u, i)
            c1 = c0 + GROUPS * G_CHUNKS

            def rows(c, k, order, start=False, stop=False, i=None):
                s = c % SLOTS
                pe.wait_ge(w_lo_ready, plus(c + 1, i, SLOTS))
                tile = bass.ds(plus(k, i, SLOTS), 1)
                for m in order:
                    if start:
                        pe.wait_ge(up_scaled, base + FT - (2 if m >= 4 else 0))
                        pe.wait_ge(hid_lo_ready, base + FT - (2 if m >= 4 else 0))
                    last = products(pe, bank[m][:, :], s, m * P, hid_hi[:, tile, :], hid_lo[:, tile, :],
                                    start, stop)
                    if stop and m < KT - 1:
                        last.then_inc(out_done, 1)
                last.then_inc(w_used, 1)

            rows(c1, 0, [4, 5, 6, 7, 0, 1, 2, 3], start=True)
            with pe.Fori(0, (FT - 2) // SLOTS) as i:
                for u in range(SLOTS):
                    rows(c1 + 1 + u, 1 + u, range(KT), i=i)
            rows(c1 + FT - 1, FT - 1, range(KT), stop=True)

        def start_load(sp):
            for i, (_, v) in enumerate(vectors):
                sp.dma_start(par_rows[(i % ROWS_A) * KT:(i % ROWS_A + 1) * KT, i // ROWS_A, :],
                             v.rearrange("(k p) -> k p", p=P)).then_inc(par_landed, 16)
            for i, v in enumerate((a["k_norm"], a["q_norm"][0])):
                row = PAR_QK - P + i * NG
                for half in range(2):
                    sp.dma_start(par_rows[row:row + NG, 1, half * HD:(half + 1) * HD], v).then_inc(par_landed, 16)
            for b in range(TB):
                sp.dma_start(x_rows[:, b, :], x_in[0, b * P:(b + 1) * P, :]).then_inc(x_landed[b], 16)

        def start_pool(pool):
            pool.memset(ident[:, :], 0.0).then_inc(id_zero, 1)
            pool.wait_ge(id_zero, 1)
            pool.affine_select(out=ident[:, :], in_=ident[:, :], compare_op=ALU.not_equal, fill=1.0, base=0,
                               pattern=[[-1, P]], channel_multiplier=1).then_inc(const_ready, 1)
            pool.memset(ones[:, :], 1.0).then_inc(const_ready, 1)

        def start_pe(pe):
            pe.wait_ge(const_ready, 2)
            for m in range(KT):
                for b in range(TB):
                    if m == 0:
                        pe.wait_ge(x_landed[b], 16)
                    last = pe.transpose(bank[m][:, b * P:(b + 1) * P], x_rows[:, b, m * P:(m + 1) * P], ident[:, :])
                last.then_inc(x_turned, 1)
            pe.wait_ge(par_landed, 16 * (len(vectors) + 4))
            pe.wait_ge(x_new, 2)
            rows_b = PAR_EXT - P
            pe.transpose(bank[0][:, 0:P], par_rows[:, 0, :], ident[:, :]).then_inc(par_turned, 1)
            pe.transpose(bank[1][:, 0:rows_b], par_rows[0:rows_b, 1, :], ident[0:rows_b, 0:rows_b]).then_inc(par_turned, 1)

        def start_act(act):
            rows_b = PAR_EXT - P
            act.wait_ge(par_turned, 2)
            act.activation(par[:, 0:P], bank[0][:, 0:P], ACT.Copy).then_inc(par_ready, 1)
            act.activation(par[:, P:P + rows_b], bank[1][:, 0:rows_b], ACT.Copy).then_inc(par_ready, 1)
            for c in range(LEAD):
                split_hi(act, c)
            act.wait_ge(par_ready, 2)

        HD = 64
        PAIRS_H = D // P
        CH = 64
        NC = T // CH
        UNITS = 2 * TB
        MIX_W, MIX_A, MIX_G, MIX_K, MIX_R, MIX_V = 1, 4, 5, 2, 0, 3
        MIXES = [MIX_W, MIX_A, MIX_G, MIX_K, MIX_R, MIX_V]
        LORA_TILES = 3 * KT
        MIX_TILES = len(MIXES) * KT
        RING = 4
        LEVELS = [1, 2, 4, 8, 16, 32]
        DECAY = float(np.exp(-0.5))

        def par_ext(i, n=1):
            return par[:, PAR_EXT + i:PAR_EXT + i + n]

        def one_minus_mu(j, k):
            return par_ext(j * KT + k)

        def one_minus_ka(k):
            return par_ext(6 * KT + k)

        def mix_act(act, n, c0):
            j, k, s = MIXES[n // KT], n % KT, n % RING
            act.wait_ge(h_ready, k + 1)
            if RING <= n < LORA_TILES + RING:
                act.wait_ge(mix_used, n - RING + 1)
            if n >= LORA_TILES + RING:
                act.wait_ge(mix_lo_ready, n - LORA_TILES - RING + 1)
            act.activation(mixed[:, s], h[:, k, 0:T], ACT.Copy, scale=col(f"mu{j}", k)).then_inc(shift_scaled, 1)

        def mix_dve(dve, n):
            j, k, s = MIXES[n // KT], n % KT, n % RING
            dve.wait_ge(shift_scaled, n + 1)
            dve.scalar_tensor_tensor(mixed[:, s], h[:, k, 1:T + 1], one_minus_mu(j, k), mixed[:, s],
                                     ALU.mult, ALU.add).then_inc(mix_ready, 1)

        def mix_hi_act(act, n, c0):
            s, t = n % RING, n - LORA_TILES
            act.wait_ge(mix_ready, n + 1)
            if t >= RING:
                act.wait_ge(w_used, c0 + t - RING + 1)
            act.activation(mix_hi[:, s], mixed[:, s], ACT.Copy).then_inc(mix_hi_ready, 1)

        def mix_lo_dve(dve, n):
            s, t = n % RING, n - LORA_TILES
            dve.wait_ge(mix_hi_ready, t + 1)
            dve.tensor_tensor(mix_lo[:, s], mixed[:, s], mix_hi[:, s].bitcast(F32),
                              ALU.subtract).then_inc(mix_lo_ready, 1)

        def rwkv_load(sp, ph):
            c0 = ph["c0"]
            for k in range(LEAD):
                load_chunk(sp, c0 + k, row_halves(a["rwkv_w_rkv"][0, 1, k * P:(k + 1) * P, :]))
            sp.wait_ge(x_new, KT * (ph["x"] + 1))
            for j, name in enumerate(("rwkv_w1", "rwkv_a1", "rwkv_g1")):
                sp.dma_start(lora1[:, j], a[name][0].rearrange("(k p) n -> p k n", p=P)).then_inc(lora_landed, 16)
            sp.wait_ge(lora_zero, 2)
            sp.dma_start(lora2[0:HD, 0], a["rwkv_w2"][0]).then_inc(lora_landed, 16)
            sp.dma_start(lora2[HD:P, 0], a["rwkv_a2"][0]).then_inc(lora_landed, 16)
            sp.dma_start(lora2[0:HD, 1], a["rwkv_g2"][0]).then_inc(lora_landed, 16)
            for i, w in enumerate([1, 0, 2]):
                for k in range(0 if i else LEAD, KT):
                    load_chunk(sp, c0 + i * KT + k, row_halves(a["rwkv_w_rkv"][0, w, k * P:(k + 1) * P, :]))
            need(sp, "y", PAIRS_H - 1)
            for k in range(KT):
                load_chunk(sp, c0 + 3 * KT + k, row_halves(a["rwkv_w_o"][0, k * P:(k + 1) * P, :]))

        def rwkv_project_act(act, ph):
            c0 = ph["c0"]
            for n in range(LORA_TILES):
                mix_act(act, n, c0)
                if n % KT == KT - 1 and n > KT:
                    lora_act(act, n // KT - 1)
            for n in range(LORA_TILES, MIX_TILES):
                mix_act(act, n, c0)
                mix_hi_act(act, n, c0)
                t = n - LORA_TILES
                if t == LEAD:
                    lora_act(act, 2)
                if t >= LEAD:
                    split_hi(act, c0 + t)
                if t >= KT + LEAD and t % KT == LEAD:
                    copy_projection(act, t // KT - 1, c0)
            copy_projection(act, 2, c0)

        def lora_act(act, j):
            act.wait_ge(mix_used, KT * (j + 1))
            act.wait_ge(lora_zero, 2)
            if j == 0:
                act.activation(lora_u[0:HD, 0], bank[0][0:HD, :], ACT.Tanh).then_inc(lora_ready, 1)
            elif j == 1:
                act.activation(lora_u[HD:P, 1], bank[1][HD:P, :], ACT.Copy).then_inc(lora_ready, 1)
            else:
                act.activation(lora_u[0:HD, 2], bank[2][0:HD, :], ACT.Sigmoid).then_inc(lora_ready, 1)

        def copy_projection(act, i, c0):
            for m in range(8):
                if m < 7:
                    act.wait_ge(projected, 7 * i + m + 1)
                else:
                    act.wait_ge(w_used, c0 + KT * (i + 1))
                if i < 2:
                    dst = (k_all, r_all)[i][:, m]
                else:
                    dst = v_all[:, m // 2, m % 2 * 512:m % 2 * 512 + 512]
                act.activation(dst, bank[m][:, :], ACT.Copy).then_inc(projection_copied, 1)

        def rwkv_project_dve(dve, ph):
            dve.tensor_scalar(par_ext(0, 6 * KT), par[:, PAR["mu0"]:PAR["mu0"] + 6 * KT], -1.0, 1.0,
                              ALU.mult, ALU.add).then_inc(ext_ready, 1)
            dve.tensor_scalar(par_ext(6 * KT, KT), par[:, PAR["rwkv_k_a"]:PAR["rwkv_k_a"] + KT], -1.0, 1.0,
                              ALU.mult, ALU.add).then_inc(ext_ready, 1)
            dve.wait_ge(x_new, KT * (ph["x"] + 1))
            dve.memset(h[:, :, 0:1], 0.0).then_inc(h_pad, 1)
            dve.memset(lora_u[:, :, :], 0.0).then_inc(lora_zero, 1)
            dve.memset(lora2[:, 1], 0.0).then_inc(lora_zero, 1)
            dve.wait_ge(h_pad, 1)
            dve.wait_ge(rstd_ready, ph["rstd"] + 1)
            for k in range(KT):
                dve.scalar_tensor_tensor(h[:, k, 1:T + 1], x[:, k], col(ph["h_gain"], k), rstd[:, :],
                                         ALU.mult, ALU.mult).then_inc(h_ready, 1)
            dve.wait_ge(ext_ready, 2)
            for n in range(MIX_TILES):
                mix_dve(dve, n)
                if n >= LORA_TILES:
                    mix_lo_dve(dve, n)

        def rwkv_project_pe(pe, ph):
            c0 = ph["c0"]
            mean_square_pe(pe, ph)
            spread_pe(pe, ph)
            pe.wait_ge(lora_landed, 16 * 6)
            pe.wait_ge(x_new, KT * (ph["x"] + 1))
            for j in range(3):
                o = bank[j][HD:P, :] if j == 1 else bank[j][0:HD, :]
                for k in range(KT):
                    pe.wait_ge(mix_ready, j * KT + k + 1)
                    last = pe.matmul(o, lora1[:, j, k], mixed[:, k % RING], start=k == 0, stop=k == KT - 1)
                    last.then_inc(mix_used, 1)
            pe.wait_ge(rstd_ready, ph["rstd"] + 1)
            for i in range(3):
                for k in range(KT):
                    t = i * KT + k
                    s, ms = (c0 + t) % SLOTS, t % RING
                    pe.wait_ge(w_lo_ready, c0 + t + 1)
                    pe.wait_ge(mix_lo_ready, t + 1)
                    for m in range(8):
                        if k == 0:
                            if i == 0:
                                pe.wait_ge(lora_ready, 3)
                            else:
                                pe.wait_ge(projection_copied, 8 * (i - 1) + m + 1)
                        if i < 2:
                            last = products(pe, bank[m][:, :], s, m * P, mix_hi[:, ms], mix_lo[:, ms],
                                            k == 0, k == KT - 1)
                        else:
                            last = products_turned(pe, bank[m][:, :], s, m % 2 * 512,
                                                   mix_hi[:, ms, m // 2 * P:m // 2 * P + P],
                                                   mix_lo[:, ms, m // 2 * P:m // 2 * P + P], k == 0, k == KT - 1)
                        if k == KT - 1 and m < 7:
                            last.then_inc(projected, 1)
                    last.then_inc(w_used, 1)

        BATCH = 4
        WORK_PRE = ["zw", "za", "norm", "inorm", "turn_b", "turn_k", "turn_v", "bonus"]
        WORK_POST = ["mean", "var", "ivar", "gate"]
        steps = rwkv_steps(PAIRS_H, len(LEVELS), NC)
        work_order = []
        for kind, q, _ in steps:
            if kind == "pre":
                work_order += [(q, w) for w in WORK_PRE]
            if kind == "units":
                work_order += [(q, f"unit{u}") for u in range(UNITS)]
            if kind == "post":
                work_order += [(q, w) for w in WORK_POST]
        work_at = {w: i for i, w in enumerate(work_order)}

        def work_bank(q, w):
            return bank[work_at[q, w] % 2]

        def work_free(pe, q, w):
            n = work_at[q, w]
            if n >= 2:
                pe.wait_ge(work_read[n % 2], n // 2)

        def work_full(eng, q, w):
            if q >= 0:
                eng.wait_ge(work_done, work_at[q, w] + 1)

        def read_work(ins, q, w):
            ins.then_inc(work_read[work_at[q, w] % 2], 1)

        def after_read(eng, q, w):
            if q >= 0:
                n = work_at[q, w]
                eng.wait_ge(work_read[n % 2], n // 2 + 1)

        def need(eng, name, q, n=None):
            per = EVENTS[name]
            if q >= 0 and per * q + (per if n is None else n) > 0:
                eng.wait_ge(S[name], per * q + (per if n is None else n))

        def done(ins, name):
            ins.then_inc(S[name], 1)

        def chunks(t):
            return t.rearrange("p (c t) -> p c t", t=CH)

        def pre_pe(pe, q, _):
            for w, j in (("zw", 0), ("za", 1)):
                work_free(pe, q, w)
                pe.matmul(work_bank(q, w)[:, :], lora2[:, 0, q * P:(q + 1) * P], lora_u[:, j],
                          start=True, stop=True).then_inc(work_done, 1)
            work_free(pe, q, "norm")
            need(pe, "sq", q)
            for b in range(TB):
                last = pe.matmul(work_bank(q, "norm")[:, 2 * b:2 * b + 2], sqt[:, b * P:(b + 1) * P], head_mask[:, 0:2],
                                 start=True, stop=True)
            last.then_inc(work_done, 1)
            spread_heads_pe(pe, q, "inorm", 1)
            for w, t, e in (("turn_b", bt, "bt"), ("turn_k", kt, "kt")):
                work_free(pe, q, w)
                need(pe, e, q)
                for b in range(TB):
                    last = pe.transpose(work_bank(q, w)[:, b * P:(b + 1) * P], t[:, b * P:(b + 1) * P], ident[:, :])
                last.then_inc(work_done, 1)
            work_free(pe, q, "turn_v")
            for b in range(TB):
                last = pe.transpose(work_bank(q, "turn_v")[:, b * P:(b + 1) * P], v_all[:, b, q * P:(q + 1) * P],
                                    ident[:, :])
            last.then_inc(work_done, 1)
            work_free(pe, q, "bonus")
            need(pe, "rk", q)
            pe.matmul(work_bank(q, "bonus")[:, :], head_ones[:, :], rk[:, :], start=True, stop=True).then_inc(work_done, 1)

        def spread_heads_pe(pe, q, w, n):
            work_free(pe, q, w)
            need(pe, ("spread_pre", "spread_post")[n - 1], q)
            for b in range(TB):
                last = pe.matmul(work_bank(q, w)[:, b * P:(b + 1) * P], spread_t[:, 2 * b:2 * b + 2, :], ident[:, :],
                                 start=True, stop=True)
            last.then_inc(work_done, 1)

        def pre_act(act, q, _):
            work_full(act, q, "zw")
            need(act, "scan_p", q - 1)
            read_work(act.activation(dec[:, :], work_bank(q, "zw")[:, :], ACT.Sigmoid, bias=col("rwkv_w0", q)), q, "zw")
            work_full(act, q, "za")
            work_full(act, q - 1, f"unit{UNITS - 1}")
            read_work(act.activation(bt[:, :], work_bank(q, "za")[:, :], ACT.Sigmoid, bias=col("rwkv_a0", q)), q, "za")
            need(act, "kkr", q)
            last_sq_use(act, q)
            done(act.activation(sqt[:, :], kkr[:, :], ACT.Square), "sq")
            after_read(act, q, "zw")
            done(act.activation(kt[:, :], dec[:, :], ACT.Exp, scale=DECAY), "undecay")
            need(act, "undecay", q)
            done(act.activation(dec[:, :], dec[:, :], ACT.Exp, scale=-DECAY), "decay")
            work_full(act, q, "norm")
            need(act, "floor", q - 1)
            read_work(act.activation(cst[:, 0, :], work_bank(q, "norm")[:, 0:8], ACT.Sqrt), q, "norm")
            if q >= 2:
                need(act, "st", q - 2)
            read_work_copy(act, q, "turn_b", btok[:, q % 2])
            read_work_copy(act, q, "turn_k", ktok[:, q % 2])
            after_read(act, q - 1, "bonus")
            read_work_copy(act, q, "turn_v", vt[:, :])

        def read_work_copy(act, q, w, dst):
            work_full(act, q, w)
            read_work(act.activation(dst, work_bank(q, w)[:, :], ACT.Copy), q, w)

        def last_sq_use(act, q):
            before = [w for w in work_order[:work_at[q, "norm"]] if w[1] in ("var", "norm")]
            if before:
                work_full(act, *before[-1])

        def spread_source_dve(dve, q, row, n):
            before = [w for w in work_order[:work_at[q, "inorm" if n == 1 else "ivar"]] if w[1] in ("inorm", "ivar")]
            if before:
                work_full(dve, *before[-1])
            done(dve.tensor_copy(spread_t[:, :, :], cst[:, row, :].unsqueeze(2).to_broadcast([P, 8, HD])),
                 ("spread_pre", "spread_post")[n - 1])

        def pre_dve(dve, q, _):
            need(dve, "sq", q - 1)
            need(dve, "ar", q - 1)
            need(dve, "kka", q - 1)
            done(dve.tensor_scalar(kkr[:, :], k_all[:, q], col("rwkv_k_k", q), None, ALU.mult), "kkr")
            need(dve, "pend", q - 1)
            need(dve, "decay", q)
            for c in range(NC):
                done(dve.tensor_tensor_scan(pcum[:, c, 1:CH + 1], dec[:, c * CH:(c + 1) * CH], ones[:, 0:CH],
                                            1.0, ALU.mult, ALU.mult), "scan_p")
            for c in range(NC):
                done(dve.tensor_tensor_scan(kt[:, c * CH:(c + 1) * CH], kt[:, c * CH:(c + 1) * CH], ones[:, 0:CH],
                                            1.0, ALU.mult, ALU.mult), "scan_r")
            after_read(dve, q, "norm")
            need(dve, "inv", q - 1)
            done(dve.tensor_scalar(cst[:, 1, :], cst[:, 0, :], 1e-12, None, ALU.max), "floor")
            need(dve, "floor", q)
            need(dve, "spread_pre", q - 1)
            done(dve.reciprocal(cst[:, 2, :], cst[:, 1, :]), "inv")
            need(dve, "inv", q)
            spread_source_dve(dve, q, 2, 1)
            work_full(dve, q, "inorm")
            need(dve, "kkr", q)
            need(dve, "sq", q)
            read_work(dve.tensor_tensor(kkr[:, :], kkr[:, :], work_bank(q, "inorm")[:, :], ALU.mult), q, "inorm")
            after_read(dve, q, "za")
            after_read(dve, q, "inorm")
            work_full(dve, q - 1, "bonus")
            done(dve.tensor_scalar(rk[:, :], bt[:, :], col("rwkv_k_a", q), one_minus_ka(q), ALU.mult, ALU.add), "tk")
            need(dve, "scan_p", q)
            if q >= 2:
                need(dve, "y", q - 2)
            for hh in range(2):
                done(dve.scalar_tensor_tensor(chunks(ar[:, q % 2, hh, 0]), pcum[:, :, 0:CH], head_mask[:, 2 + hh:3 + hh],
                                              chunks(kkr[:, :]), ALU.mult, ALU.mult), "ar")
                done(dve.scalar_tensor_tensor(chunks(ar[:, q % 2, hh, 1]), pcum[:, :, 1:CH + 1], head_mask[:, hh:hh + 1],
                                              chunks(r_all[:, q]), ALU.mult, ALU.mult), "ar")
            if q >= 2:
                need(dve, "state", q - 2)
            done(dve.tensor_copy(pend[:, q % 2, :], pcum[:, :, CH]), "pend")
            need(dve, "kp", q)
            done(dve.scalar_tensor_tensor(rk[:, :], r_all[:, q], col("rwkv_r_k", q), k_all[:, q],
                                          ALU.mult, ALU.mult), "rk")
            work_full(dve, q, "bonus")
            after_read(dve, q, "turn_v")
            if q >= 2:
                need(dve, "biased", q - 2)
            read_work(dve.tensor_tensor(bonus_v[:, q % 2], work_bank(q, "bonus")[:, :], vt[:, :], ALU.mult), q, "bonus")

        def pre_pool(pool, q, _):
            need(pool, "tk", q)
            done(pool.tensor_tensor(k_all[:, q], k_all[:, q], rk[:, :], ALU.mult), "kp")
            after_read(pool, q, "inorm")
            done(pool.tensor_tensor(bt[:, :], bt[:, :], kkr[:, :], ALU.mult), "kka")
            need(pool, "scan_r", q)
            need(pool, "kka", q)
            done(pool.tensor_tensor(bt[:, :], bt[:, :], kt[:, :], ALU.mult), "bt")
            need(pool, "kp", q)
            need(pool, "bt", q)
            done(pool.tensor_tensor(kt[:, :], k_all[:, q], kt[:, :], ALU.mult), "kt")

        def units_pe(pe, q, _):
            need(pe, "ar", q)
            for u in range(UNITS):
                hh, b = u // TB, u % TB
                blk = slice(b * P, (b + 1) * P)
                work_free(pe, q, f"unit{u}")
                o = work_bank(q, f"unit{u}")
                rhs = ar[:, q % 2, hh, :, blk]
                pe.matmul(o[:, 0:256], bt[:, blk], rhs, start=True, stop=True)
                pe.matmul(o[:, 256:512], kt[:, blk], rhs, start=True, stop=True).then_inc(work_done, 1)
            for v in range(2):
                need(pe, "first", q, v + 1)
                need(pe, "us", q - 1)
                for u in range(BATCH):
                    last = pe.transpose(bank[2 + v][:, u * P:(u + 1) * P], inv_u[:, q % 2, v * BATCH + u, :], ident[:, :])
                done(last, "t")

        def units_act(act, q, _):
            for v in range(2):
                turn_x_act(act, q, v, 0)

        def turn_x_act(act, q, v, l):
            need(act, "t", q, 2 * l + v + 1)
            if l == 0:
                need(act, "g", q - 1)
            done(act.activation(inv_x[:, v], bank[2 + v][:, :].rearrange("p (u t) -> p u t", t=P), ACT.Copy), "x")

        def units_dve(dve, q, _):
            for u in range(UNITS):
                work_full(dve, q, f"unit{u}")
                if u == 0:
                    need(dve, "y", q - 2)
                    need(dve, "us", q - 1)
                read_work(dve.tensor_tensor(am[:, q % 2, u, :], work_bank(q, f"unit{u}")[:, :], unit_mask[:, :],
                                            ALU.mult), q, f"unit{u}")
            for v in range(2):
                us = slice(v * BATCH, (v + 1) * BATCH)
                after_read(dve, q, f"unit{v * BATCH + BATCH - 1}")
                after_read(dve, q, f"unit{v * BATCH + BATCH - 2}")
                done(dve.tensor_tensor(inv_u[:, q % 2, us, :], am[:, q % 2, us, 0:P],
                                       level_mask[:, 0:1, :].to_broadcast([P, BATCH, P]), ALU.mult), "firstm")
                need(dve, "firstm", q, v + 1)
                done(dve.tensor_tensor(inv_u[:, q % 2, us, :], inv_u[:, q % 2, us, :],
                                       ident[:, :].unsqueeze(1).to_broadcast([P, BATCH, P]), ALU.add), "first")

        def level_pe(pe, q, l):
            for v in range(2):
                need(pe, "x", q, 2 * (l - 1) + v + 1)
                for u in range(BATCH):
                    last = pe.matmul(bank[2 + v][:, u * P:(u + 1) * P], am[:, q % 2, v * BATCH + u, 0:P],
                                     inv_x[:, v, u, :], start=True, stop=True)
                done(last, "g")
            for v in range(2):
                need(pe, "gs", q, 2 * (l - 1) + v + 1)
                for u in range(BATCH):
                    last = pe.matmul(bank[2 + v][:, u * P:(u + 1) * P], inv_g[:, v, u, :],
                                     inv_u[:, q % 2, v * BATCH + u, :], start=True, stop=True)
                done(last, "u")
            if l < len(LEVELS) - 1:
                for v in range(2):
                    need(pe, "us", q, 2 * (l - 1) + v + 1)
                    for u in range(BATCH):
                        last = pe.transpose(bank[2 + v][:, u * P:(u + 1) * P], inv_u[:, q % 2, v * BATCH + u, :],
                                            ident[:, :])
                    done(last, "t")

        def level_act(act, q, l):
            if l < len(LEVELS) - 1:
                for v in range(2):
                    turn_x_act(act, q, v, l)

        def level_dve(dve, q, l):
            for v in range(2):
                need(dve, "g", q, 2 * (l - 1) + v + 1)
                done(dve.tensor_tensor(inv_g[:, v], bank[2 + v][:, :].rearrange("p (u t) -> p u t", t=P),
                                       level_mask[:, l:l + 1, :].to_broadcast([P, BATCH, P]), ALU.mult), "gs")
            for v in range(2):
                us = slice(v * BATCH, (v + 1) * BATCH)
                need(dve, "u", q, 2 * (l - 1) + v + 1)
                done(dve.tensor_tensor(inv_u[:, q % 2, us, :], inv_u[:, q % 2, us, :],
                                       bank[2 + v][:, :].rearrange("p (u t) -> p u t", t=P), ALU.add), "us")

        def scan_pe(pe, q, c):
            b, o = c // 2, c % 2 * CH
            rows = slice(o, o + CH)
            if c == 0:
                need(pe, "us", q)
                after_read(pe, q, "turn_k")
                after_read(pe, q, "turn_b")
            if c > 0:
                need(pe, "state", q, c)
            for hh in range(2):
                u, dst = hh * TB + b, bank[4][rows, hh * HD:(hh + 1) * HD]
                if c > 0:
                    pe.matmul(dst, ar[:, q % 2, hh, 0, b * P + o:b * P + o + CH], state[:, c % 2, :], start=True, stop=False)
                last = pe.matmul(dst, am[:, q % 2, u, 256 + o:256 + o + CH],
                                 v_all[:, b, q * P + hh * HD:q * P + (hh + 1) * HD], start=c == 0, stop=True)
            done(last, "z")
            need(pe, "zs", q, c + 1)
            for hh in range(2):
                last = pe.matmul(bank[5][rows, hh * HD:(hh + 1) * HD], inv_u[:, q % 2, hh * TB + b, rows],
                                 zs[:, hh * HD:(hh + 1) * HD], start=True, stop=True)
            done(last, "sa")
            if c < NC - 1:
                for hh in range(2):
                    pe.matmul(bank[6][hh * HD:(hh + 1) * HD, 0:HD], ktok[rows, q % 2, b * P + hh * HD:b * P + (hh + 1) * HD],
                              v_all[rows, b, q * P + hh * HD:q * P + (hh + 1) * HD], start=True, stop=False)
                    if hh == 0:
                        need(pe, "sas", q, c + 1)
                    last = pe.matmul(bank[6][hh * HD:(hh + 1) * HD, 0:HD],
                                     btok[rows, q % 2, b * P + hh * HD:b * P + (hh + 1) * HD],
                                     sas[rows, hh * HD:(hh + 1) * HD], start=False, stop=True)
                done(last, "st")
            else:
                need(pe, "sas", q, c + 1)
            if c == 0:
                need(pe, "ys", q - 1)
            for hh in range(2):
                u, dst = hh * TB + b, bank[7][hh * HD:(hh + 1) * HD, c * CH:(c + 1) * CH]
                if c > 0:
                    pe.matmul(dst, state[:, c % 2, :], ar[:, q % 2, hh, 1, b * P + o:b * P + o + CH], start=True, stop=False)
                pe.matmul(dst, v_all[:, b, q * P + hh * HD:q * P + (hh + 1) * HD], am[:, q % 2, u, 384 + o:384 + o + CH],
                          start=c == 0, stop=False)
                last = pe.matmul(dst, sas[rows, hh * HD:(hh + 1) * HD], am[rows, q % 2, u, 128 + o:128 + o + CH],
                                 start=False, stop=True)
            done(last, "y")

        def scan_act(act, q, c):
            rows = slice(c % 2 * CH, c % 2 * CH + CH)
            need(act, "z", q, c + 1)
            done(act.activation(zs[rows, :], bank[4][rows, 0:2 * HD], ACT.Copy), "zs")
            need(act, "sa", q, c + 1)
            need(act, "y", q, c - 1)
            done(act.activation(sas[rows, :], bank[5][rows, 0:2 * HD], ACT.Copy), "sas")

        def scan_dve(dve, q, c):
            if c == NC - 1:
                return
            p_end = pend[:, q % 2, c:c + 1]
            if c > 0:
                need(dve, "state", q, c)
                done(dve.tensor_scalar(decayed[:, :], state[:, c % 2, :], p_end, None, ALU.mult), "decayed")
                need(dve, "decayed", q, c)
            need(dve, "st", q, c + 1)
            need(dve, "y", q, c)
            nxt = state[:, (c + 1) % 2, :]
            if c == 0:
                need(dve, "y", q - 1)
                need(dve, "pend", q)
                done(dve.tensor_scalar(nxt, bank[6][:, 0:HD], p_end, None, ALU.mult), "state")
            else:
                done(dve.scalar_tensor_tensor(nxt, bank[6][:, 0:HD], p_end, decayed[:, :], ALU.mult, ALU.add), "state")

        def post_pe(pe, q, _):
            work_free(pe, q, "mean")
            need(pe, "ys", q)
            pe.matmul(work_bank(q, "mean")[:, :], head_mean[:, :], ys[:, :], start=True, stop=True).then_inc(work_done, 1)
            work_free(pe, q, "var")
            need(pe, "ysq", q)
            for b in range(TB):
                last = pe.matmul(work_bank(q, "var")[:, 2 * b:2 * b + 2], sqt[:, b * P:(b + 1) * P], head_mask[:, 0:2],
                                 start=True, stop=True)
            last.then_inc(work_done, 1)
            spread_heads_pe(pe, q, "ivar", 2)
            work_free(pe, q, "gate")
            pe.matmul(work_bank(q, "gate")[:, :], lora2[:, 1, q * P:(q + 1) * P], lora_u[:, 2],
                      start=True, stop=True).then_inc(work_done, 1)

        def post_act(act, q, _):
            need(act, "y", q)
            need(act, "y_lo", q - 1)
            done(act.activation(ys[:, :], bank[7][:, :], ACT.Copy), "ys")
            after_read(act, q, "mean")
            before = [w for w in work_order[:work_at[q, "var"]] if w[1] in ("var", "norm")]
            work_full(act, *before[-1])
            done(act.activation(sqt[:, :], ys[:, :], ACT.Square), "ysq")
            need(act, "ginv", q)
            need(act, "spread_post", q - 1)
            done(act.activation(cst[:, 5, :], cst[:, 4, :], ACT.Sqrt), "groot")
            after_read(act, q, "ivar")
            done(act.activation(ys[:, :], ys[:, :], ACT.Identity, bias=col("rwkv_ln_b", q), scale=col("rwkv_ln_w", q)), "yl")
            after_read(act, q, "gate")
            need(act, "rk", q)
            done(act.activation(y_hi[:, q], ys[:, :], ACT.Copy), "y_hi")

        def post_dve(dve, q, _):
            work_full(dve, q, "mean")
            read_work(dve.tensor_tensor(ys[:, :], ys[:, :], work_bank(q, "mean")[:, :], ALU.subtract), q, "mean")
            work_full(dve, q, "var")
            need(dve, "ginv", q - 1)
            read_work(dve.tensor_scalar(cst[:, 3, :], work_bank(q, "var")[:, 0:8], 1.0 / HD, GN_EPS, ALU.mult, ALU.add), q, "var")
            after_read(dve, q, "var")
            need(dve, "groot", q - 1)
            done(dve.reciprocal(cst[:, 4, :], cst[:, 3, :]), "ginv")
            need(dve, "groot", q)
            spread_source_dve(dve, q, 5, 2)
            work_full(dve, q, "ivar")
            after_read(dve, q, "mean")
            need(dve, "ysq", q)
            read_work(dve.tensor_tensor(ys[:, :], ys[:, :], work_bank(q, "ivar")[:, :], ALU.mult), q, "ivar")
            need(dve, "yl", q)
            after_read(dve, q, "bonus")
            done(dve.tensor_tensor(ys[:, :], ys[:, :], bonus_v[:, q % 2], ALU.add), "biased")
            need(dve, "biased", q)
            work_full(dve, q, "gate")
            ins = dve.tensor_tensor(ys[:, :], ys[:, :], work_bank(q, "gate")[:, :], ALU.mult)
            read_work(ins, q, "gate")
            after_read(dve, q, "gate")
            need(dve, "y_hi", q)
            done(dve.tensor_tensor(y_lo[:, q], ys[:, :], y_hi[:, q].bitcast(F32), ALU.subtract), "y_lo")

        STEP_PE = dict(pre=pre_pe, units=units_pe, level=level_pe, scan=scan_pe, post=post_pe)
        STEP_ACT = dict(pre=pre_act, units=units_act, level=level_act, scan=scan_act, post=post_act)
        STEP_DVE = dict(pre=pre_dve, units=units_dve, level=level_dve, scan=scan_dve, post=post_dve)

        def pool_masks(pool):
            pool.wait_ge(projection_copied, 24)
            count = 0

            def chain(ins):
                nonlocal count
                count += 1
                ins.then_inc(mask_step, 1)
                pool.wait_ge(mask_step, count)

            chain(pool.memset(unit_mask[:, :], 1.0))
            for i in range(4):
                m = unit_mask[:, i * P:(i + 1) * P]
                chain(pool.affine_select(out=m, in_=m, compare_op=ALU.is_ge if i % 2 else ALU.is_gt, fill=0.0, base=0,
                                         pattern=[[1, P]], channel_multiplier=-1))
            chain(pool.memset(unit_mask[0:CH, :].rearrange("p (i c t) -> p i c t", i=4, c=2)[:, :, 1, :], 0.0))
            chain(pool.memset(level_mask[:, :, :], 0.0))
            m = level_mask[:, 0, :].rearrange("p (k e) -> p k e", e=2)[:, :, 1]
            chain(pool.affine_select(out=m, in_=m, compare_op=ALU.not_equal, fill=1.0, base=0, pattern=[[-2, P // 2]],
                                     channel_multiplier=1))
            for l in range(1, len(LEVELS)):
                w = LEVELS[l]
                m = level_mask[:, l, :].rearrange("p (k e r) -> p k e r", e=2, r=w)[:, :, 0, :]
                chain(pool.memset(m, 1.0))
                chain(pool.affine_select(out=m, in_=m, compare_op=ALU.is_ge, fill=0.0, base=-w,
                                         pattern=[[-2 * w, P // (2 * w)], [0, w]], channel_multiplier=1))
                chain(pool.affine_select(out=m, in_=m, compare_op=ALU.is_ge, fill=0.0, base=2 * w - 1,
                                         pattern=[[2 * w, P // (2 * w)], [0, w]], channel_multiplier=-1))
            for t, value in ((head_ones, 1.0), (head_mean, 1.0 / HD)):
                chain(pool.memset(t[:, :], 0.0))
                chain(pool.memset(t[0:HD, 0:HD], value))
                chain(pool.memset(t[HD:P, HD:P], value))
            chain(pool.memset(head_mask[:, :], 0.0))
            for i, (half, value) in enumerate([(0, 1.0), (1, 1.0), (0, -1.0), (1, -1.0)]):
                chain(pool.memset(head_mask[half * HD:(half + 1) * HD, i:i + 1], value))
            chain(pool.memset(pcum[:, :, 0:1], 1.0))
            pool.memset(zs[:, :], 0.0).then_inc(masks_ready, 1)

        def rwkv_act(act, ph):
            rwkv_project_act(act, ph)
            act.wait_ge(masks_ready, 1)
            for kind, q, n in steps:
                STEP_ACT[kind](act, q, n)
            for t in range(LEAD):
                split_hi(act, ph["c0"] + 3 * KT + t)
            split_hi_run(act, ph["c0"] + 3 * KT + LEAD, min(KT, CHUNKS - ph["c0"] - 3 * KT - LEAD))

        def rwkv_dve(dve, ph):
            rwkv_project_dve(dve, ph)
            dve.wait_ge(projection_copied, 24)
            dve.wait_ge(masks_ready, 1)
            for kind, q, n in steps:
                STEP_DVE[kind](dve, q, n)

        def rwkv_pool(pool, ph):
            split_lo_run(pool, ph["c0"] + LEAD, 3 * KT - LEAD)
            pool_masks(pool)
            for kind, q, n in steps:
                if kind == "pre":
                    pre_pool(pool, q, n)
            split_lo_run(pool, ph["c0"] + 3 * KT, min(KT + LEAD, CHUNKS - ph["c0"] - 3 * KT))

        def rwkv_pe(pe, ph):
            rwkv_project_pe(pe, ph)
            pe.wait_ge(projection_copied, 24)
            pe.wait_ge(masks_ready, 1)
            for kind, q, n in steps:
                STEP_PE[kind](pe, q, n)
            c0 = ph["c0"] + 3 * KT
            for k in range(KT):
                pe.wait_ge(w_lo_ready, c0 + k + 1)
                if k == 0:
                    need(pe, "y_lo", PAIRS_H - 1)
                for m in range(KT):
                    last = products(pe, bank[m][:, :], (c0 + k) % SLOTS, m * P, y_hi[:, k], y_lo[:, k],
                                    k == 0, k == KT - 1)
                    if k == KT - 1 and m < KT - 1:
                        last.then_inc(out_done, 1)
                last.then_inc(w_used, 1)

        COLS = 512
        HALVES = D // COLS
        QKV_CHUNKS = KT // 2
        KEYS_GROUPS = NG * HALVES

        def tokens(g, b):
            return slice(b * P, (b + 1) * P) if g == 0 else slice(b, T, TB)

        def rs_col(g, b):
            return stat[:, 2, (TB if g else 0) + b:(TB if g else 0) + b + 1]

        KV_GROUPS = [("k", g, hf) for g in range(NG) for hf in range(HALVES)] + \
                    [("v", g, hf) for g in range(NG) for hf in range(HALVES)]
        Q_GROUPS = [("q", g, hf) for g in range(NG) for hf in range(HALVES)]
        NORMED = {("k", g, hf): g * HALVES + hf for g in range(NG) for hf in range(HALVES)}
        NORMED.update({("q", g, hf): KEYS_GROUPS + g * HALVES + hf for g in range(NG) for hf in range(HALVES)})

        def qkv_source(kind, g, hf, j):
            w, first = (a["attn_w_q"][0], 0) if kind == "q" else (a["w_kv"], 0 if kind == "k" else NG * D)
            first += g * D + hf * COLS
            return [(w[(2 * j + kk) * P:(2 * j + kk + 1) * P, first:first + COLS],
                     lambda slot, kk=kk: slot[:, kk * COLS:(kk + 1) * COLS]) for kk in range(2)]

        def qkv_load(sp, ph):
            n_v = 0
            for gi, grp in enumerate(ph["groups"]):
                for j in range(QKV_CHUNKS):
                    load_chunk(sp, ph["c0"] + gi * QKV_CHUNKS + j, qkv_source(*grp, j))
                if gi >= 2:
                    store_group(sp, ph, gi - 2)

        def store_group(sp, ph, gi):
            kind, g, hf = ph["groups"][gi]
            if kind == "k":
                n = NORMED[kind, g, hf]
                sp.wait_ge(staged_even, 2 * (n + 1))
                sp.wait_ge(staged_odd, 2 * (n + 1))
                sp.dma_start(k_dram[g, hf * 4:(hf + 1) * 4].rearrange("q p t -> p q t"),
                             stage[:, gi % 2]).then_inc(stored[gi % 2], 16)
            elif kind == "v":
                n = g * HALVES + hf
                sp.wait_ge(v_even, 2 * (n + 1))
                sp.wait_ge(v_odd, 2 * (n + 1))
                sp.dma_start(v_dram[g, :, :, hf * COLS:(hf + 1) * COLS].rearrange("b p n -> p b n"),
                             stage[:, gi % 2]).then_inc(stored[gi % 2], 16)

        def banks_free(pe, ph, gi, b):
            if gi < 2:
                return
            kind, g, hf = ph["groups"][gi - 2]
            even, odd = (v_even, v_odd) if kind == "v" else (staged_even, staged_odd)
            n = g * HALVES + hf if kind == "v" else NORMED[kind, g, hf]
            pe.wait_ge(odd if b % 2 else even, 2 * n + b // 2 + 1)

        def turn_group_pe(pe, ph, gi):
            if gi < 0 or ph["groups"][gi][0] == "v":
                return
            n = NORMED[ph["groups"][gi]]
            for b in range(TB):
                pe.wait_ge(group_normed, TB * n + b + 1)
                for r in range(4):
                    last = pe.transpose(bank[4 * (gi % 2) + b][:, r * P:(r + 1) * P], raw[:, b, r * P:(r + 1) * P],
                                        ident[:, :])
                last.then_inc(group_turned, 1)

        def qkv_pe(pe, ph):
            for gi, grp in enumerate(ph["groups"]):
                for j in range(QKV_CHUNKS):
                    c = ph["c0"] + gi * QKV_CHUNKS + j
                    pe.wait_ge(w_lo_ready, c + 1)
                    for kk in range(2):
                        k = 2 * j + kk
                        if gi == 0:
                            pe.wait_ge(xg_lo_ready, KT * ph["prep"] + k + 1)
                        for b in range(TB):
                            if k == 0:
                                if gi == 0:
                                    pe.wait_ge(x_new, KT * ph["x"] + b + 1)
                                banks_free(pe, ph, gi, b)
                            ts = tokens(grp[1], b)
                            last = products_turned(pe, bank[4 * (gi % 2) + b][:, :], c % SLOTS, kk * COLS,
                                                   xg_hi[:, k, ts], xg_lo[:, k, ts], k == 0, k == KT - 1)
                    last.then_inc(w_used, 1)
                    if gi == 0 and j == 2:
                        mean_square_pe(pe, ph)
                    if gi == 0 and j == 3:
                        spread_pe(pe, ph)
                        pe.wait_ge(rstd_ready, ph["rstd"] + 1)
                    if j == 1:
                        turn_group_pe(pe, ph, gi - 1)
            turn_group_pe(pe, ph, len(ph["groups"]) - 1)

        def qkv_act(act, ph):
            act.wait_ge(root_ready, ph["stat"] + 1)
            for gi, (kind, g, hf) in enumerate(ph["groups"]):
                end = ph["c0"] + (gi + 1) * QKV_CHUNKS
                for j in range(QKV_CHUNKS):
                    if end - QKV_CHUNKS + LEAD + j < CHUNKS:
                        split_hi(act, end - QKV_CHUNKS + LEAD + j)
                act.wait_ge(w_used, end)
                if kind == "v":
                    n = g * HALVES + hf
                    if gi >= 2:
                        act.wait_ge(stored[gi % 2], 16 * stores_before(ph, gi))
                    for b in range(0, TB, 2):
                        act.activation(stage[:, gi % 2, b], bank[4 * (gi % 2) + b][:, :], ACT.Copy,
                                       scale=rs_col(g, b)).then_inc(v_even, 1)
                    continue
                n = NORMED[kind, g, hf]
                for b in range(TB):
                    if n > 0:
                        act.wait_ge(group_turned, TB * (n - 1) + b + 1)
                    act.activation(raw[:, b], bank[4 * (gi % 2) + b][:, :], ACT.Copy,
                                   scale=rs_col(g, b)).then_inc(group_raw, 1)
                for b in range(TB):
                    act.wait_ge(group_raw, TB * n + b + 1)
                    if TB * n + b >= 2:
                        act.wait_ge(group_summed, TB * n + b - 1)
                    act.activation(raw_sq[:, b % 2], raw[:, b], ACT.Square).then_inc(group_squared, 1)
                act.wait_ge(group_inv, n + 1)
                act.activation(group_stat[:, 3, :], group_stat[:, 2, :], ACT.Sqrt).then_inc(group_root, 1)
                for b in range(0, TB, 2):
                    act.wait_ge(group_turned, TB * n + b + 1)
                    if kind == "k" and gi >= 2 and b == 0:
                        act.wait_ge(stored[gi % 2], 16 * stores_before(ph, gi))
                    act.activation(*group_place(kind, g, hf, gi, b), ACT.Copy, **gain_of(kind, g)).then_inc(staged_even, 1)

        def stores_before(ph, gi):
            return sum(1 for i in range(gi) if i % 2 == gi % 2)

        def gain_of(kind, g):
            return dict(scale=par_ext(7 * KT + g)) if kind == "k" else {}

        def group_place(kind, g, hf, gi, b):
            src = bank[4 * (gi % 2) + b][:, :].rearrange("p (q t) -> p q t", t=P)
            if kind == "k":
                return stage[:, gi % 2, :, b * P:(b + 1) * P], src
            return q_all[:, hf * 4:(hf + 1) * 4, g, b * P:(b + 1) * P], src

        def qkv_dve(dve, ph):
            if ph["groups"] is KV_GROUPS:
                dve.scalar_tensor_tensor(par_ext(7 * KT, NG), par[:, PAR_QK:PAR_QK + NG], float(HD) ** -0.5,
                                         par[:, PAR_QK + NG:PAR_QK + 2 * NG], ALU.mult, ALU.mult).then_inc(gains_ready, 1)
                dve.wait_ge(gains_ready, 1)
            for gi, (kind, g, hf) in enumerate(ph["groups"]):
                end = ph["c0"] + (gi + 1) * QKV_CHUNKS
                if kind == "v":
                    dve.wait_ge(w_used, end)
                    dve.wait_ge(stored[gi % 2], 16 * stores_before(ph, gi))
                    for b in range(1, TB, 2):
                        dve.tensor_scalar(stage[:, gi % 2, b], bank[4 * (gi % 2) + b][:, :], rs_col(g, b), None,
                                          ALU.mult).then_inc(v_odd, 1)
                    continue
                n = NORMED[kind, g, hf]
                for b in range(TB):
                    dve.wait_ge(group_squared, TB * n + b + 1)
                    dve.tensor_reduce(group_stat[:, 0, b * 8:(b + 1) * 8],
                                      raw_sq[:, b % 2].rearrange("p (h d) -> p h d", d=HD), AX.X,
                                      ALU.add).then_inc(group_summed, 1)
                dve.wait_ge(group_summed, TB * (n + 1))
                dve.tensor_scalar(group_stat[:, 1, :], group_stat[:, 0, :], 1.0 / HD, EPS, ALU.mult,
                                  ALU.add).then_inc(group_var, 1)
                dve.wait_ge(group_var, n + 1)
                if n > 0:
                    dve.wait_ge(group_root, n)
                dve.reciprocal(group_stat[:, 2, :], group_stat[:, 1, :]).then_inc(group_inv, 1)
                dve.wait_ge(group_root, n + 1)
                for b in range(TB):
                    dve.tensor_tensor(raw[:, b].rearrange("p (h d) -> p h d", d=HD),
                                      raw[:, b].rearrange("p (h d) -> p h d", d=HD),
                                      group_stat[:, 3, b * 8:(b + 1) * 8].unsqueeze(2).to_broadcast([P, 8, HD]),
                                      ALU.mult).then_inc(group_normed, 1)
                for b in range(1, TB, 2):
                    dve.wait_ge(group_turned, TB * n + b + 1)
                    if kind == "k" and gi >= 2 and b == 1:
                        dve.wait_ge(stored[gi % 2], 16 * stores_before(ph, gi))
                    dst, src = group_place(kind, g, hf, gi, b)
                    if kind == "k":
                        i = dve.tensor_scalar(dst, src, par_ext(7 * KT + g), None, ALU.mult)
                    else:
                        i = dve.tensor_copy(dst, src)
                    i.then_inc(staged_odd, 1)

        def qkv_pool(pool, ph):
            c = ph["c0"] + LEAD
            n = min(len(ph["groups"]) * QKV_CHUNKS, CHUNKS - c)
            if ph["groups"] is KV_GROUPS:
                split_lo_run(pool, c, n)
                return
            steps = attn_mask_steps(pool)
            pool.wait_ge(x_new, KT * (ph["x"] + 1))
            for t in range(max(n, len(steps))):
                if t < n:
                    split_lo(pool, c + t)
                if t < len(steps):
                    if t < n:
                        pool.wait_ge(w_lo_ready, c + t + 1)
                    steps[t]().then_inc(attn_mask_step, 1)
                    pool.wait_ge(attn_mask_step, t + 1)

        UNITS_A = [(q, f, hh) for q in range(PAIRS_H) for f in range(2) for hh in range(2)]
        NU = len(UNITS_A)

        def attn_mask_steps(pool):
            causal, band = masks_f[:, 0], masks_f[:, 1]
            res = [lambda: pool.memset(masks_f[:, :, :], 0.0),
                   lambda: pool.memset(select[:, :, :], 0.0),
                   lambda: pool.memset(head_half[:, :], 0.0),
                   lambda: pool.affine_select(out=causal, in_=causal, compare_op=ALU.is_ge, fill=NEG, base=0,
                                              pattern=[[-1, P]], channel_multiplier=1),
                   lambda: pool.affine_select(out=band, in_=band, compare_op=ALU.is_ge, fill=NEG, base=0,
                                              pattern=[[1, P]], channel_multiplier=-1)]
            for hh in range(2):
                res.append(lambda hh=hh: pool.memset(head_half[hh * HD:(hh + 1) * HD, hh:hh + 1], 1.0))
            for b in range(TB):
                sel = select[:, b].rearrange("p (j r) -> p j r", r=TB)
                res.append(lambda b=b, sel=sel: pool.affine_select(
                    out=sel, in_=sel, compare_op=ALU.not_equal, fill=1.0, base=-b * (P // TB),
                    pattern=[[-1, P // TB], [0, TB]], channel_multiplier=1))
            return res

        MASK_STEPS = 7 + TB

        def attn_consts_dve(dve):
            dve.wait_ge(attn_mask_step, MASK_STEPS)
            n = 0

            def chain(ins):
                nonlocal n
                n += 1
                ins.then_inc(attn_const, 1)
                dve.wait_ge(attn_const, n)

            chain(dve.tensor_reduce(onehot[:, :], ident[:, :].rearrange("p (j r) -> p r j", r=TB), AX.X, ALU.add))
            chain(dve.tensor_scalar(penalty[:, :], onehot[:, :], -NEG, NEG, ALU.mult, ALU.add))
            chain(dve.tensor_tensor(masks_f[:, 2].rearrange("p (j r) -> p j r", r=TB),
                                    masks_f[:, 0].rearrange("p (j r) -> p j r", r=TB),
                                    penalty[:, :].unsqueeze(1).to_broadcast([P, P // TB, TB]), ALU.add))
            chain(dve.tensor_copy(ident_bf[:, :], ident[:, :]))
            causal, band, dilated = range(3)
            for i, parts in enumerate([(None, causal, band, causal), (band, causal, band, causal),
                                       (causal, dilated) * 2, (causal, dilated) * 2]):
                for j, part in enumerate(parts):
                    dst = masks_bf[:, i, j * P:(j + 1) * P]
                    chain(dve.memset(dst, NEG) if part is None else dve.tensor_copy(dst, masks_f[:, part]))

        ATTN_CONSTS = 4 + 16

        def attn_load(sp, ph):
            qkv_load(sp, ph)
            for k in range(SLOTS):
                load_wo(sp, ph, k)
            sp.wait_ge(w_used, ph["c0"] + len(Q_GROUPS) * QKV_CHUNKS)
            for q in range(PAIRS_H):
                if q >= 2:
                    sp.wait_ge(pv_done, 4 * (q - 1))
                for g in range(NG):
                    sp.dma_start(keys[:, q % 2, g], k_dram[g, q]).then_inc(keys_landed[q % 2][g], 16)
                    sp.dma_start(values[:, q % 2, g], v_dram[g, :, :, q * P:(q + 1) * P].rearrange("b p n -> p b n")
                                 ).then_inc(values_landed[q % 2][g], 16)
            for k in range(SLOTS, KT):
                load_wo(sp, ph, k)

        def load_wo(sp, ph, k):
            load_chunk(sp, ph["c0"] + len(Q_GROUPS) * QKV_CHUNKS + k, row_halves(a["attn_w_o"][0, k * P:(k + 1) * P, :]))

        def scores_pe(pe, i):
            q, f, hh = UNITS_A[i]
            if f == 0 and hh == 0:
                for g in range(NG):
                    pe.wait_ge(keys_landed[q % 2][g], 16 * (q // 2 + 1))
                pe.wait_ge(q_padded, 6 * (q + 1))
            for half in range(2):
                o = bank[2 * (i % 2) + half]
                if i >= 2:
                    pe.wait_ge(p_ready, 4 * (i - 2) + 2 * half + 2)
                pe.matmul(o[:, :], ident_bf[:, :], masks_bf[:, 2 * f + half], start=True, stop=False)
                for b in (2 * half, 2 * half + 1):
                    dst = o[:, (b % 2) * 256:(b % 2) * 256 + 256]
                    blk = slice(b * P, (b + 1) * P)
                    if f == 0 and b == 0:
                        last = pe.matmul(dst[:, P:256], q_pad[:, q % 2, 0, hh, blk], keys[:, q % 2, 0, 0:P],
                                         start=False, stop=False)
                    elif f == 0:
                        last = pe.matmul(dst, q_pad[:, q % 2, 0, hh, blk], keys[:, q % 2, 0, (b - 1) * P:(b + 1) * P],
                                         start=False, stop=b % 2 == 1)
                    else:
                        pe.matmul(dst[:, 0:P], q_pad[:, q % 2, 1, hh, blk], keys[:, q % 2, 1, blk], start=False, stop=False)
                        last = pe.matmul(dst[:, P:256], q_pad[:, q % 2, 2, hh, blk], keys[:, q % 2, 2, blk],
                                         start=False, stop=b % 2 == 1)
                last.then_inc(scores_done, 1)

        def turn_pe(pe, i):
            for half in range(2):
                if i >= 1:
                    pe.wait_ge(turn_read[half], i)
                pe.wait_ge(p_ready, 4 * i + 2 * half + 2)
                for n in range(4):
                    last = pe.transpose(bank[4 + half][:, n * P:(n + 1) * P],
                                        probs[:, i % 2, 2 * half + n // 2, n % 2 * P:n % 2 * P + P], ident[:, :])
                last.then_inc(turn_done[half], 1)

        def pv_pe(pe, i):
            q, f, hh = UNITS_A[i]
            if hh == 0:
                if q >= 1:
                    pe.wait_ge(u_copied[f], q)
                for g in ([0] if f == 0 else [1, 2]):
                    pe.wait_ge(values_landed[q % 2][g], 16 * (q // 2 + 1))
            for b in range(TB):
                if b % 2 == 0:
                    pe.wait_ge(turn_read[b // 2], i + 1)
                dst = bank[6 + f][hh * HD:(hh + 1) * HD, b * P:(b + 1) * P]
                for kb in range(2):
                    if f == 0:
                        if b == 0 and kb == 0:
                            continue
                        v = values[:, q % 2, 0, b - 1 + kb, hh * HD:(hh + 1) * HD]
                    else:
                        v = values[:, q % 2, 1 + kb, b, hh * HD:(hh + 1) * HD]
                    last = pe.matmul(dst, v, probs_t[:, i % 2, 2 * b + kb], start=kb == 0 or (f == 0 and b == 0),
                                     stop=kb == 1)
            last.then_inc(pv_done, 1)

        def attn_pe(pe, ph):
            qkv_pe(pe, ph)
            pe.wait_ge(staged_odd, 2 * 2 * KEYS_GROUPS)
            pe.wait_ge(staged_even, 2 * 2 * KEYS_GROUPS)
            pe.wait_ge(attn_const, ATTN_CONSTS)
            for i in range(NU + 2):
                if i < NU:
                    scores_pe(pe, i)
                if i >= 2:
                    pv_pe(pe, i - 2)
                if 1 <= i <= NU:
                    turn_pe(pe, i - 1)
            pe.wait_ge(turn_read[0], NU)
            for b in range(TB):
                last = pe.matmul(bank[4][:, b * P:(b + 1) * P], select[:, b], sums[:, 1].rearrange("p b s h -> p (b s h)"),
                                 start=True, stop=True)
            last.then_inc(converted, 1)
            for q in range(PAIRS_H):
                pe.wait_ge(spread_source, 2 * (q + 1))
                if q >= 2:
                    pe.wait_ge(weighted, 3 * (q - 1))
                for f in range(2):
                    for b in range(TB):
                        last = pe.matmul(bank[2 * (q % 2) + f][:, b * P:(b + 1) * P], spread_w[:, q % 2, f, b],
                                         ident[:, :], start=True, stop=True)
                last.then_inc(w_spread, 1)
            c0 = ph["c0"] + len(Q_GROUPS) * QKV_CHUNKS
            for k in range(KT):
                pe.wait_ge(w_lo_ready, c0 + k + 1)
                if k == 0:
                    pe.wait_ge(o_lo_ready, KT)
                for m in range(KT):
                    last = products(pe, bank[m][:, :], (c0 + k) % SLOTS, m * P, o_hl[:, k, 0], o_hl[:, k, 1],
                                    k == 0, k == KT - 1)
                    if k == KT - 1 and m < KT - 1:
                        last.then_inc(out_done, 1)
                last.then_inc(w_used, 1)

        def attn_act(act, ph):
            qkv_act(act, ph)
            for i in range(NU + 2):
                if i < NU:
                    q, f, hh = UNITS_A[i]
                    for b in range(TB):
                        act.wait_ge(negmax_ready, 2 * i + b // 2 + 1)
                        if i >= 2 and b % 2 == 0:
                            act.wait_ge(turn_done[b // 2], i - 1)
                        src = bank[2 * (i % 2) + b // 2][:, (b % 2) * 256:(b % 2) * 256 + 256]
                        head = 2 * q + hh
                        act.activation(probs[:, i % 2, b], src, ACT.Exp, bias=sums[:, f, b, 0, head:head + 1],
                                       accum_out=sums[:, f, b, 1, head:head + 1]).then_inc(p_ready, 1)
                if i >= 2:
                    q, f, hh = UNITS_A[i - 2]
                    if hh == 1:
                        act.wait_ge(pv_done, i - 1)
                        src, dst = bank[6 + f][:, :], q_all[:, q, f, :]
                        if f == 1:
                            src = src.rearrange("p (r m) -> p m r", r=TB)
                            dst = dst.rearrange("p (m r) -> p m r", r=TB)
                        act.activation(dst, src, ACT.Copy).then_inc(u_copied[f], 1)
                if 1 <= i <= NU:
                    act.wait_ge(turn_done[0], i)
                    if i >= 3:
                        act.wait_ge(pv_done, i - 2)
                    act.activation(probs_t[:, (i - 1) % 2, 0:4], bank[4][:, :].rearrange("p (n t) -> p n t", t=P),
                                   ACT.Copy).then_inc(turn_read[0], 1)
            act.wait_ge(merged, 4)
            act.activation(joint[:, 3:5], joint[:, 1:3], ACT.Exp).then_inc(exps_ready, 1)
            c = ph["c0"] + len(Q_GROUPS) * QKV_CHUNKS + LEAD
            for q in range(PAIRS_H):
                act.wait_ge(weighted, 3 * (q + 1))
                act.activation(o_hl[:, q, 0], q_all[:, q, 0], ACT.Copy).then_inc(o_hi_ready, 1)
                if q == 0 and c < CHUNKS:
                    split_hi(act, c)
            split_hi_run(act, c + 1, min(KT - 1, CHUNKS - c - 1))

        def attn_dve(dve, ph):
            qkv_dve(dve, ph)
            attn_consts_dve(dve)
            dve.wait_ge(group_turned, TB * 2 * KEYS_GROUPS)
            dve.wait_ge(staged_even, 2 * 2 * KEYS_GROUPS)
            dve.wait_ge(staged_odd, 2 * 2 * KEYS_GROUPS)

            def pad(q):
                for g in range(NG):
                    for hh in range(2):
                        dve.tensor_scalar(q_pad[:, q % 2, g, hh], q_all[:, q, g], head_half[:, hh:hh + 1], None,
                                          ALU.mult).then_inc(q_padded, 1)

            pad(0)
            for i in range(NU + 1):
                if i < NU:
                    q, f, hh = UNITS_A[i]
                    for half in range(2):
                        dve.wait_ge(scores_done, 2 * i + half + 1)
                        dve.tensor_reduce(sums[:, f, 2 * half:2 * half + 2, 0, 2 * q + hh],
                                          bank[2 * (i % 2) + half][:, :].rearrange("p (b k) -> p b k", b=2),
                                          AX.X, ALU.max, negate=True).then_inc(negmax_ready, 1)
                    if i % 4 == 1 and q + 1 < PAIRS_H:
                        pad(q + 1)
                if i >= 1:
                    dve.wait_ge(turn_done[1], i)
                    if i >= 3:
                        dve.wait_ge(pv_done, i - 2)
                    dve.tensor_copy(probs_t[:, (i - 1) % 2, 4:8], bank[5][:, :].rearrange("p (n t) -> p n t", t=P)
                                    ).then_inc(turn_read[1], 1)
            dve.wait_ge(converted, 1)
            for b in range(TB):
                dve.tensor_tensor(picked[:, b], bank[4][:, b * P:(b + 1) * P].rearrange("p (r c) -> p c r", r=TB),
                                  onehot[:, :].unsqueeze(1).to_broadcast([P, 2 * HEADS, TB]), ALU.mult
                                  ).then_inc(picked_done, 1)
            dve.wait_ge(picked_done, TB)
            dve.tensor_reduce(turned[:, :, :], picked[:, :, :, :], AX.X, ALU.add).then_inc(merged, 1)
            dve.wait_ge(merged, 1)
            neg0, sum0 = sums[:, 0, :, 0, :], sums[:, 0, :, 1, :]
            neg1, sum1 = turned[:, :, 0:HEADS], turned[:, :, HEADS:2 * HEADS]
            dve.tensor_tensor(joint[:, 0], neg0, neg1, ALU.min).then_inc(merged, 1)
            dve.wait_ge(merged, 2)
            dve.tensor_tensor(joint[:, 1], joint[:, 0], neg0, ALU.subtract).then_inc(merged, 1)
            dve.tensor_tensor(joint[:, 2], joint[:, 0], neg1, ALU.subtract).then_inc(merged, 1)
            dve.wait_ge(exps_ready, 1)
            dve.tensor_tensor(joint[:, 5], joint[:, 3], sum0, ALU.mult).then_inc(merged, 1)
            dve.tensor_tensor(joint[:, 6], joint[:, 4], sum1, ALU.mult).then_inc(merged, 1)
            dve.wait_ge(merged, 6)
            dve.tensor_tensor(joint[:, 5], joint[:, 5], joint[:, 6], ALU.add).then_inc(merged, 1)
            dve.wait_ge(merged, 7)
            dve.reciprocal(joint[:, 7], joint[:, 5]).then_inc(merged, 1)
            dve.wait_ge(merged, 8)
            for f in range(2):
                dve.tensor_tensor(joint[:, 1 + f], joint[:, 3 + f], joint[:, 7], ALU.mult).then_inc(merged, 1)
            dve.wait_ge(merged, 10)

            def spread(q):
                for f in range(2):
                    dve.tensor_copy(spread_w[:, q % 2, f], joint[:, 1 + f, :, 2 * q:2 * q + 2].unsqueeze(3).to_broadcast(
                        [P, TB, 2, HD])).then_inc(spread_source, 1)

            spread(0)
            spread(1)
            for q in range(PAIRS_H):
                dve.wait_ge(w_spread, q + 1)
                for f in range(2):
                    dve.tensor_tensor(q_all[:, q, f], q_all[:, q, f], bank[2 * (q % 2) + f][:, :],
                                      ALU.mult).then_inc(weighted, 1)
                if q + 2 < PAIRS_H:
                    spread(q + 2)
                dve.wait_ge(weighted, 3 * q + 2)
                dve.tensor_tensor(q_all[:, q, 0], q_all[:, q, 0], q_all[:, q, 1], ALU.add).then_inc(weighted, 1)
                dve.wait_ge(o_hi_ready, q + 1)
                dve.tensor_tensor(o_hl[:, q, 1], q_all[:, q, 0], o_hl[:, q, 0].bitcast(F32),
                                  ALU.subtract).then_inc(o_lo_ready, 1)

        def attn_pool(pool, ph):
            qkv_pool(pool, ph)
            c = ph["c0"] + LEAD + len(Q_GROUPS) * QKV_CHUNKS
            split_lo_run(pool, c, min(KT, CHUNKS - c))

        def end_pe(pe, ph):
            for b in range(TB):
                for m in range(KT):
                    if b == 0:
                        pe.wait_ge(x_new, KT * ph["x"] + m + 1)
                    last = pe.transpose(bank[2 * b + m // 4][:, (m % 4) * P:(m % 4 + 1) * P],
                                        x[:, m, b * P:(b + 1) * P], ident[:, :])
                last.then_inc(y_turned, 1)

        def end_act(act, ph):
            for b in range(TB):
                act.wait_ge(y_turned, b + 1)
                act.activation(x_rows[:, b, 0:512], bank[2 * b][:, :], ACT.Copy).then_inc(y_ready, 1)

        def end_dve(dve, ph):
            for b in range(TB):
                dve.wait_ge(y_turned, b + 1)
                dve.tensor_copy(x_rows[:, b, 512:1024], bank[2 * b + 1][:, :]).then_inc(y_right_ready, 1)

        def end_store(sp, ph):
            for b in range(TB):
                sp.wait_ge(y_ready, b + 1)
                sp.wait_ge(y_right_ready, b + 1)
                sp.dma_start(out[0, b * P:(b + 1) * P, :], x_rows[:, b, :]).then_inc(y_stored, 16)
            sp.wait_ge(y_stored, 16 * TB)

        def ffn(n, scale):
            return dict(n=n, gain=f"ffn{n // 2}{n % 2}", scale=scale, stats=1, chunks=FFN_CHUNKS,
                        load=ffn_load, act=ffn_act, pool=ffn_pool, dve=ffn_dve, pe=ffn_pe)

        def nothing(engine, ph):
            pass

        mix0 = dict(gain=None, h_gain="mix0", scale=0.5, stats=1, chunks=4 * KT, load=rwkv_load, act=rwkv_act,
                    dve=rwkv_dve, pe=rwkv_pe, pool=rwkv_pool)
        kv = dict(gain="kv_norm", scale=0.5, stats=1, groups=KV_GROUPS, chunks=len(KV_GROUPS) * QKV_CHUNKS,
                  load=qkv_load, act=qkv_act, dve=qkv_dve, pe=qkv_pe, pool=qkv_pool)
        ffn2 = ffn(2, 1.0)
        ffn2["stats"] = 0
        del ffn2["scale"]
        attn = dict(gain="mix1", scale=0.5, stats=1, groups=Q_GROUPS, chunks=len(Q_GROUPS) * QKV_CHUNKS + KT,
                    load=attn_load, act=attn_act, dve=attn_dve, pe=attn_pe, pool=attn_pool)
        plan = [ffn(0, 1.0), mix0, ffn(1, 1.0), kv, ffn2, attn, ffn(3, 1.0)][lo:upto]
        plan += [dict(gain=None, scale=0.5 if "n" in plan[-1] else 1.0, stats=0, chunks=0)]
        c, u, p, st, ffns = 0, 0, 0, 0, 0
        for ph in plan:
            ph["c0"] = c
            c += ph["chunks"]
            if "scale" in ph:
                ph["update"] = ph["x"] = u
                u += 1
            else:
                ph["update"], ph["x"] = None, u - 1
            ph["stat"] = st if ph["stats"] else None
            st += ph["stats"]
            ph["rstd"] = st - 1
            ph["prep"] = p if ph["gain"] else None
            p += bool(ph["gain"])
            ph["nth"] = ffns
            ffns += "n" in ph
        CHUNKS = c

        block = ctx.enter_context(nc.Block())

        @block.sync
        def _(sp):
            start_load(sp)
            for ph in plan:
                ph.get("load", nothing)(sp, ph)
            end_store(sp, plan[-1])

        @block.gpsimd
        def _(pool):
            start_pool(pool)
            for c in range(LEAD):
                split_lo(pool, c)
            for ph in plan:
                ph.get("pool", nothing)(pool, ph)

        @block.scalar
        def _(act):
            start_act(act)
            for ph in plan:
                update_act(act, ph)
                if ph["stat"] is not None:
                    rstd_act(act, ph)
                ph.get("act", nothing)(act, ph)
            end_act(act, plan[-1])

        @block.vector
        def _(dve):
            for ph in plan:
                update_dve(dve, ph)
                if ph["stat"] is not None:
                    rstd_dve(dve, ph)
                ph.get("dve", nothing)(dve, ph)
            end_dve(dve, plan[-1])

        @block.tensor
        def _(pe):
            start_pe(pe)
            for ph in plan:
                ph.get("pe", nothing)(pe, ph)
            end_pe(pe, plan[-1])


_INS = ["x", "ffn_norm", "ffn_w_in", "ffn_w_out", "mix_norm", "rwkv_mu", "rwkv_w_rkv", "rwkv_w0", "rwkv_w1",
        "rwkv_w2", "rwkv_a0", "rwkv_a1", "rwkv_a2", "rwkv_g1", "rwkv_g2", "rwkv_k_k", "rwkv_k_a", "rwkv_r_k",
        "rwkv_ln_w", "rwkv_ln_b", "rwkv_w_o", "kv_norm", "w_kv", "k_norm", "attn_w_q", "q_norm", "attn_w_o"]


def kernel(**inputs):
    import concourse.bacc as bacc
    from concourse.bass_utils import run_bass_kernel_spmd

    nc = bacc.Bacc("TRN2", target_bir_lowering=False, num_devices=1)
    arrays, args = {}, {}
    for name in _INS:
        arrays[f"in_{name}"] = np.ascontiguousarray(inputs[name])
        args[name] = nc.dram_tensor(f"in_{name}", arrays[f"in_{name}"].shape, F32, kind="ExternalInput").ap()
    out = nc.dram_tensor("out_x", inputs["x"].shape, F32, kind="ExternalOutput").ap()
    build(nc, args, out)
    return run_bass_kernel_spmd(nc, [arrays], core_ids=[0]).results[0]["out_x"]
```
